# Optimizing a Trainium2 kernel written in Bass

```python
import math
import jax
import jax.numpy as jnp
from jax import lax
import numpy as np

D_MODEL = 1024
BATCH = 1
SEQ = 256
DEPTH = 2

CTX_LEN = 256
GRID_W = 64
EPS = 1e-6
ROPE_BASE = 10000.0

DN_HEADS = 6
DN_DK = 64
DN_DV = 64
DN_CONV = 5
DN_CHUNK = 64
DA_HEADS = 4
DA_QK = 32
DA_V = 64
WA_HEADS = 6
WA_KV_HEADS = 2
WA_DIM = 64
WINDOW = 128
BLOCK = 128
BANDK = BLOCK + 2 * WINDOW

A_QK_W = DN_HEADS * DN_DK
A_W = DN_HEADS * DN_DV
B_W = DA_HEADS * DA_V
C_W = WA_HEADS * WA_DIM
MIX_W = A_W + B_W + C_W
A_COLS = 2 * A_QK_W + 2 * A_W + 4 * DN_HEADS
B_COLS = 4 * DA_HEADS * DA_QK + B_W
C_COLS = C_W + 2 * WA_KV_HEADS * WA_DIM
IN_COLS = A_COLS + B_COLS + C_COLS

N_GROUPS = 4
EXP_PER_GROUP = 4
N_EXPERTS = N_GROUPS * EXP_PER_GROUP
TOP_K = 2
D_EXPERT = 512

kernel_name = 'hybrid_deltanet_diffattn_swa_hmoe_dit'

def rms_norm(x, g):
    xf = x.astype(jnp.float32)
    y = xf * lax.rsqrt(jnp.mean(xf * xf, axis=-1, keepdims=True) + EPS)
    return (y * g.astype(jnp.float32)).astype(x.dtype)

def l2_normalize(x):
    return x * lax.rsqrt(jnp.sum(x * x, axis=-1, keepdims=True) + EPS)

def axial_rope_tables(row, col, dim):
    nf = dim // 4
    inv = ROPE_BASE ** (-jnp.arange(nf, dtype=jnp.float32) / nf)
    ang = jnp.stack([row[:, None] * inv, col[:, None] * inv], axis=1)
    return jnp.cos(ang), jnp.sin(ang)

def apply_rope(x, cos, sin):
    b, l, h, dim = x.shape
    xr = x.reshape(b, l, h, 2, 2, dim // 4)
    x1, x2 = xr[..., 0, :], xr[..., 1, :]
    c = cos[None, :, None].astype(x.dtype)
    s = sin[None, :, None].astype(x.dtype)
    return jnp.stack([x1 * c - x2 * s, x2 * c + x1 * s], axis=-2).reshape(b, l, h, dim)

def short_conv(u, w):
    k = w.shape[0]
    return lax.conv_general_dilated(
        u, w[:, None, :].astype(u.dtype), window_strides=(1,), padding=[(k // 2, k // 2)],
        dimension_numbers=('NWC', 'WIO', 'NWC'), feature_group_count=u.shape[-1])

def gated_delta_chunked(q, k, v, g, beta, s0):
    bn, l, h, dk = q.shape
    dv = v.shape[-1]
    C = DN_CHUNK
    n = l // C

    def chunk(t):
        return jnp.moveaxis(t.reshape((bn, n, C) + t.shape[2:]), 3, 1)

    q, k, v, g, beta = chunk(q), chunk(k), chunk(v), chunk(g), chunk(beta)
    gc = jnp.cumsum(g, axis=-1)
    idx = jnp.arange(C)
    tril = idx[:, None] >= idx[None, :]
    strict = idx[:, None] > idx[None, :]
    diff = gc[..., :, None] - gc[..., None, :]
    decay = jnp.where(tril, jnp.exp(jnp.where(tril, diff, 0.0)), 0.0)
    kb = k * beta[..., None]
    a_mat = jnp.where(strict, jnp.einsum('bhncd,bhnsd->bhncs', kb, k) * decay, 0.0)
    eye = jnp.eye(C, dtype=q.dtype)
    rhs = jnp.concatenate([v * beta[..., None], kb * jnp.exp(gc)[..., None]], axis=-1)
    sol = lax.linalg.triangular_solve(eye + a_mat, rhs, left_side=True, lower=True)
    u, w = sol[..., :dv], sol[..., dv:]
    attn = jnp.einsum('bhncd,bhnsd->bhncs', q, k) * decay
    q_dec = q * jnp.exp(gc)[..., None]
    g_last = gc[..., -1]
    k_dec = k * jnp.exp(g_last[..., None] - gc)[..., None]

    def step(S, inp):
        qd, kd, ui, wi, ai, gl = inp
        v_new = ui - jnp.einsum('bhcd,bhde->bhce', wi, S)
        o = jnp.einsum('bhcd,bhde->bhce', qd, S) + jnp.einsum('bhcs,bhse->bhce', ai, v_new)
        S = S * jnp.exp(gl)[..., None, None] + jnp.einsum('bhcd,bhce->bhde', kd, v_new)
        return S, o

    xs = tuple(jnp.moveaxis(t, 2, 0) for t in (q_dec, k_dec, u, w, attn, g_last))
    S, o = lax.scan(step, s0, xs)
    o = jnp.transpose(o, (1, 0, 3, 2, 4)).reshape(bn, l, h, dv)
    return o, S

def dn_prepare(z, conv_w, a_log, dt_bias):
    b, l, _ = z.shape
    h = DN_HEADS
    qkv_w = 2 * A_QK_W + A_W
    qkv = jax.nn.silu(short_conv(z[..., :qkv_w], conv_w)).astype(jnp.float32)
    q = l2_normalize(qkv[..., :A_QK_W].reshape(b, l, h, DN_DK)) * (DN_DK ** -0.5)
    k = l2_normalize(qkv[..., A_QK_W:2 * A_QK_W].reshape(b, l, h, DN_DK))
    v = qkv[..., 2 * A_QK_W:].reshape(b, l, h, DN_DV)
    gate = z[..., qkv_w:qkv_w + A_W]
    ab = z[..., qkv_w + A_W:].astype(jnp.float32).reshape(b, l, 2, 2, h)
    g = -jnp.exp(a_log.astype(jnp.float32)) * jax.nn.softplus(ab[:, :, 0] + dt_bias.astype(jnp.float32))
    beta = jax.nn.sigmoid(ab[:, :, 1])

    def dirs(t_f, t_b):
        return jnp.concatenate([t_f, jnp.flip(t_b, axis=1)], axis=0)

    return (dirs(q, q), dirs(k, k), dirs(v, v), dirs(g[:, :, 0], g[:, :, 1]),
            dirs(beta[:, :, 0], beta[:, :, 1])), gate

def dn_finish(o, gate, norm_g):
    b = o.shape[0] // 2
    l = o.shape[1]
    o = o[:b] + jnp.flip(o[b:], axis=1)
    o = rms_norm(o, norm_g) * jax.nn.silu(gate.astype(jnp.float32).reshape(b, l, DN_HEADS, DN_DV))
    return o.reshape(b, l, A_W).astype(gate.dtype)

def deltanet_mixer(z, zc, conv_w, a_log, dt_bias, norm_g, ctx_out):
    lat, gate = dn_prepare(z, conv_w, a_log, dt_bias)
    cin, gate_c = dn_prepare(zc, conv_w, a_log, dt_bias)
    s0 = jnp.zeros((2 * z.shape[0], DN_HEADS, DN_DK, DN_DV), jnp.float32)
    o_c, s_c = gated_delta_chunked(*cin, s0)
    o, _ = gated_delta_chunked(*lat, s_c)
    y = dn_finish(o, gate, norm_g)
    yc = dn_finish(o_c, gate_c, norm_g) if ctx_out else None
    return y, yc

def diff_core(q1, q2, k1, k2, v, lam):
    scale = DA_QK ** -0.5
    p1 = jax.nn.softmax(jnp.einsum('bhqd,bhkd->bhqk', q1, k1).astype(jnp.float32) * scale, axis=-1)
    p2 = jax.nn.softmax(jnp.einsum('bhqd,bhkd->bhqk', q2, k2).astype(jnp.float32) * scale, axis=-1)
    return jnp.einsum('bhqk,bhkd->bhqd', (p1 - lam * p2).astype(v.dtype), v)

def diff_attention(z, zc, cos, sin, lam_vecs, subln_g, layer_idx, ctx_out):
    b, l, _ = z.shape
    h = DA_HEADS
    qk_w = 2 * h * DA_QK

    def heads(zz, rope):
        bb, n = zz.shape[0], zz.shape[1]
        q = zz[..., :qk_w].reshape(bb, n, 2 * h, DA_QK)
        k = zz[..., qk_w:2 * qk_w].reshape(bb, n, 2 * h, DA_QK)
        v = zz[..., 2 * qk_w:].reshape(bb, n, h, DA_V)
        if rope:
            q = apply_rope(q, cos, sin)
            k = apply_rope(k, cos, sin)

        def halves(t):
            return jnp.transpose(t, (0, 2, 1, 3)).reshape(bb, h, 2, n, DA_QK)

        return halves(q), halves(k), jnp.transpose(v, (0, 2, 1, 3))

    lv = lam_vecs.astype(jnp.float32)
    lam_init = 0.8 - 0.6 * math.exp(-0.3 * layer_idx)
    lam = jnp.exp(jnp.sum(lv[0] * lv[1])) - jnp.exp(jnp.sum(lv[2] * lv[3])) + lam_init
    q, k, v = heads(z, True)
    qc, kc, vc = heads(zc, False)
    k_all = jnp.concatenate([k, kc], axis=3)
    v_all = jnp.concatenate([v, vc], axis=2)
    nb = l // BLOCK
    qb = jnp.moveaxis(q.reshape(b, h, 2, nb, BLOCK, DA_QK), 3, 0)
    o = lax.map(lambda qj: diff_core(qj[:, :, 0], qj[:, :, 1], k_all[:, :, 0], k_all[:, :, 1], v_all, lam), qb)
    o = jnp.moveaxis(o, 0, 2).reshape(b, h, l, DA_V)

    def finish(t):
        t = rms_norm(jnp.transpose(t, (0, 2, 1, 3)), subln_g) * (1.0 - lam_init)
        return t.reshape(t.shape[0], t.shape[1], B_W)

    y = finish(o)
    yc = finish(diff_core(qc[:, :, 0], qc[:, :, 1], kc[:, :, 0], kc[:, :, 1], vc, lam)) if ctx_out else None
    return y, yc

def sink_attend(scores, values, sink):
    s = jnp.concatenate([t.astype(jnp.float32) for t in scores], axis=-1)
    sk = sink[None, :, :, None, None]
    m = jnp.maximum(jnp.max(s, axis=-1, keepdims=True), sk)
    e = jnp.exp(s - m)
    p = e / (jnp.sum(e, axis=-1, keepdims=True) + jnp.exp(sk - m))
    v = jnp.concatenate(values, axis=1)
    return jnp.einsum('bgrqk,bkgd->bqgrd', p.astype(v.dtype), v)

def window_attention(z, zc, cos, sin, sink, ctx_out):
    b, l, _ = z.shape
    g, r = WA_KV_HEADS, WA_HEADS // WA_KV_HEADS
    kv_w = g * WA_DIM
    scale = WA_DIM ** -0.5

    def heads(zz):
        bb, n = zz.shape[0], zz.shape[1]
        q = zz[..., :C_W].reshape(bb, n, WA_HEADS, WA_DIM)
        k = zz[..., C_W:C_W + kv_w].reshape(bb, n, g, WA_DIM)
        v = zz[..., C_W + kv_w:].reshape(bb, n, g, WA_DIM)
        return q, k, v

    q, k, v = heads(z)
    q = apply_rope(q, cos, sin)
    k = apply_rope(k, cos, sin)
    qc, kc, vc = heads(zc)
    sink_f = sink.astype(jnp.float32).reshape(g, r)
    nb = l // BLOCK
    pad = ((0, 0), (WINDOW, WINDOW), (0, 0), (0, 0))
    kp, vp = jnp.pad(k, pad), jnp.pad(v, pad)
    qb = jnp.moveaxis((q * scale).reshape(b, nb, BLOCK, g, r, WA_DIM), 1, 0)
    rel = jnp.arange(BANDK)[None, :] - jnp.arange(BLOCK)[:, None]
    band = (rel >= 0) & (rel <= 2 * WINDOW)

    def block(args):
        qj, j = args
        start = j * BLOCK
        kj = lax.dynamic_slice_in_dim(kp, start, BANDK, axis=1)
        vj = lax.dynamic_slice_in_dim(vp, start, BANDK, axis=1)
        pos = start - WINDOW + jnp.arange(BANDK)
        mask = band & ((pos >= 0) & (pos < l))[None, :]
        s_loc = jnp.where(mask, jnp.einsum('bqgrd,bkgd->bgrqk', qj, kj).astype(jnp.float32), -jnp.inf)
        s_ctx = jnp.einsum('bqgrd,bcgd->bgrqc', qj, kc)
        return sink_attend([s_loc, s_ctx], [vj, vc], sink_f)

    o = lax.map(block, (qb, jnp.arange(nb)))
    y = jnp.moveaxis(o, 0, 1).reshape(b, l, C_W)
    yc = None
    if ctx_out:
        lc = qc.shape[1]
        qcs = (qc * scale).reshape(b, lc, g, r, WA_DIM)
        yc = sink_attend([jnp.einsum('bqgrd,bcgd->bgrqc', qcs, kc)], [vc], sink_f).reshape(b, lc, C_W)
    return y, yc

def hier_moe(h, wg, bg, we, be, w_gate, w_up, w_down):
    lg = (h @ wg).astype(jnp.float32) + bg.astype(jnp.float32)
    pg = jax.nn.softmax(lg, axis=-1)
    oh_g = jax.nn.one_hot(jnp.argmax(lg, axis=-1), N_GROUPS, dtype=jnp.float32)
    p_sel = jnp.sum(pg * oh_g, axis=-1)
    le = ((h @ we).astype(jnp.float32) + be.astype(jnp.float32)).reshape(-1, N_GROUPS, EXP_PER_GROUP)
    le_sel = jnp.einsum('ng,nge->ne', oh_g, le)
    top_v, top_i = lax.top_k(le_sel, TOP_K)
    top_w = jax.nn.softmax(top_v, axis=-1)
    within = jnp.einsum('nk,nke->ne', top_w, jax.nn.one_hot(top_i, EXP_PER_GROUP, dtype=jnp.float32))
    gate = ((oh_g * p_sel[:, None])[:, :, None] * within[:, None, :]).reshape(-1, N_EXPERTS).astype(h.dtype)
    out = jnp.zeros_like(h)
    for e in range(N_EXPERTS):
        hid = jax.nn.silu(h @ w_gate[e]) * (h @ w_up[e])
        out = out + gate[:, e, None] * (hid @ w_down[e])
    return out

def setup_inputs(seed: int = 0) -> dict:
    key = jax.random.key(seed)
    ks = jax.random.split(key, 32)
    f32 = jnp.float32

    def nrm(k, shape, s):
        return jax.random.normal(k, shape, f32) * s

    dt = jnp.exp(jax.random.uniform(ks[10], (DEPTH, 2, DN_HEADS), f32, math.log(1e-3), math.log(1e-1)))
    return {
        'x': nrm(ks[0], (BATCH, SEQ, D_MODEL), 1.0),
        'c': nrm(ks[1], (BATCH, D_MODEL), 1.0),
        'ctx': nrm(ks[2], (BATCH, CTX_LEN, D_MODEL), 1.0),
        'c_ctx': nrm(ks[3], (D_MODEL,), 1.0),
        'ada_w': nrm(ks[4], (DEPTH, D_MODEL, 6 * D_MODEL), 0.5 * D_MODEL ** -0.5),
        'ada_b': nrm(ks[5], (DEPTH, 6 * D_MODEL), 0.02),
        'norm1_g': 1.0 + nrm(ks[6], (DEPTH, D_MODEL), 0.05),
        'norm2_g': 1.0 + nrm(ks[7], (DEPTH, D_MODEL), 0.05),
        'w_in': nrm(ks[8], (DEPTH, D_MODEL, IN_COLS), D_MODEL ** -0.5),
        'dn_conv_w': nrm(ks[9], (DEPTH, DN_CONV, 2 * A_QK_W + A_W), DN_CONV ** -0.5),
        'dn_a_log': jnp.log(jax.random.uniform(ks[11], (DEPTH, 2, DN_HEADS), f32, 1.0, 16.0)),
        'dn_dt_bias': dt + jnp.log(-jnp.expm1(-dt)),
        'dn_norm_g': 1.0 + nrm(ks[12], (DEPTH, DN_DV), 0.05),
        'da_lambda': nrm(ks[13], (DEPTH, 4, DA_QK), 0.1),
        'da_subln_g': 1.0 + nrm(ks[14], (DEPTH, DA_V), 0.05),
        'wa_sink': nrm(ks[15], (DEPTH, WA_HEADS), 1.0),
        'w_out': nrm(ks[16], (DEPTH, MIX_W, D_MODEL), MIX_W ** -0.5),
        'router_group_w': nrm(ks[17], (DEPTH, D_MODEL, N_GROUPS), D_MODEL ** -0.5),
        'router_group_b': nrm(ks[18], (DEPTH, N_GROUPS), 0.01),
        'router_expert_w': nrm(ks[19], (DEPTH, D_MODEL, N_EXPERTS), D_MODEL ** -0.5),
        'router_expert_b': nrm(ks[20], (DEPTH, N_EXPERTS), 0.01),
        'exp_w_gate': nrm(ks[21], (DEPTH, N_EXPERTS, D_MODEL, D_EXPERT), D_MODEL ** -0.5),
        'exp_w_up': nrm(ks[22], (DEPTH, N_EXPERTS, D_MODEL, D_EXPERT), D_MODEL ** -0.5),
        'exp_w_down': nrm(ks[23], (DEPTH, N_EXPERTS, D_EXPERT, D_MODEL), D_EXPERT ** -0.5),
        'final_norm_g': 1.0 + nrm(ks[24], (D_MODEL,), 0.05),
    }

def reference(x, c, ctx, c_ctx, ada_w, ada_b, norm1_g, norm2_g, w_in, dn_conv_w, dn_a_log, dn_dt_bias,
              dn_norm_g, da_lambda, da_subln_g, wa_sink, w_out, router_group_w, router_group_b,
              router_expert_w, router_expert_b, exp_w_gate, exp_w_up, exp_w_down, final_norm_g):
    b, l, d = x.shape
    lc = ctx.shape[1]
    rows = l // GRID_W
    row = jnp.repeat(jnp.arange(rows, dtype=jnp.float32), GRID_W)
    col = jnp.tile(jnp.arange(GRID_W, dtype=jnp.float32), rows)
    cos_b, sin_b = axial_rope_tables(row, col, DA_QK)
    cos_w, sin_w = axial_rope_tables(row, col, WA_DIM)
    s1, s2 = A_COLS, A_COLS + B_COLS
    xc = ctx
    for li in range(DEPTH):
        last = li == DEPTH - 1
        sh1, sc1, g1, sh2, sc2, g2 = jnp.split((jax.nn.silu(c) @ ada_w[li] + ada_b[li])[:, None, :], 6, axis=-1)
        sh1c, sc1c, g1c, sh2c, sc2c, g2c = jnp.split(jax.nn.silu(c_ctx) @ ada_w[li] + ada_b[li], 6, axis=-1)
        h = rms_norm(x, norm1_g[li]) * (1.0 + sc1) + sh1
        hc = rms_norm(xc, norm1_g[li]) * (1.0 + sc1c) + sh1c
        z = h @ w_in[li]
        zc = hc @ w_in[li]
        ya, yac = deltanet_mixer(z[..., :s1], zc[..., :s1], dn_conv_w[li], dn_a_log[li], dn_dt_bias[li],
                                 dn_norm_g[li], not last)
        yb, ybc = diff_attention(z[..., s1:s2], zc[..., s1:s2], cos_b, sin_b, da_lambda[li], da_subln_g[li],
                                 li, not last)
        yw, ywc = window_attention(z[..., s2:], zc[..., s2:], cos_w, sin_w, wa_sink[li], not last)
        x = x + g1 * (jnp.concatenate([ya, yb, yw], axis=-1) @ w_out[li])
        h2 = rms_norm(x, norm2_g[li]) * (1.0 + sc2) + sh2
        moe_w = (router_group_w[li], router_group_b[li], router_expert_w[li], router_expert_b[li],
                 exp_w_gate[li], exp_w_up[li], exp_w_down[li])
        if not last:
            xc = xc + g1c * (jnp.concatenate([yac, ybc, ywc], axis=-1) @ w_out[li])
            h2c = rms_norm(xc, norm2_g[li]) * (1.0 + sc2c) + sh2c
            tokens = jnp.concatenate([h2.reshape(b * l, d), h2c.reshape(b * lc, d)], axis=0)
            ff = hier_moe(tokens, *moe_w)
            x = x + g2 * ff[:b * l].reshape(b, l, d)
            xc = xc + g2c * ff[b * l:].reshape(b, lc, d)
        else:
            x = x + g2 * hier_moe(h2.reshape(b * l, d), *moe_w).reshape(b, l, d)
    return rms_norm(x, final_norm_g)


_drawn_inputs = setup_inputs


def setup_inputs(seed=0):
    import zlib

    import numpy as np

    out = dict(_drawn_inputs(seed))
    spreads = {}
    factors = {'norm1_g': 2.854,
     'dn_norm_g': 5.884,
     'da_lambda': 8.0,
     'da_subln_g': 14.242,
     'wa_sink': 64.0,
     'router_group_b': 42.315,
     'router_expert_b': 53.659,
     'norm2_g': 5.997}
    for name, (base, spread) in spreads.items():
        noise = np.random.default_rng([zlib.crc32(name.encode()), seed]).standard_normal(out[name].shape)
        drawn = base * np.exp(spread * noise) if base else spread * noise
        out[name] = jnp.asarray(drawn.astype(out[name].dtype))
    for name, factor in factors.items():
        out[name] = (out[name] * factor).astype(out[name].dtype)
    return out
```

```python
import math
from contextlib import ExitStack

import numpy as np

import concourse.bass as bass
from concourse import mybir
from concourse.alu_op_type import AluOpType as ALU

P = 128
D = 1024
KD = D // P
SEQ, CTX = 256, 256
TILES = (SEQ + CTX) // P
LAT_TILES = SEQ // P
DEPTH = 2
EPS = 1e-6
GRID_W = 64
ROPE_BASE = 10000.0

DN_H, DN_D, TAPS = 6, 64, 5
DA_H, DA_QK, DA_V = 4, 32, 64
WA_H, WA_KV, WA_D = 6, 2, 64
WINDOW = 128
DN_W = DN_H * DN_D
QKV_CH = 3 * DN_W // P
COL_GATE = 3 * DN_W
COL_AB = COL_GATE + DN_W
COL_ATT = COL_AB + 4 * DN_H
GAB_W = DN_W + 4 * DN_H
DAQK_W = 4 * DA_H * DA_QK
DAV_W = DA_H * DA_V
WAQ_W, WAKV_W = WA_H * WA_D, 2 * WA_KV * WA_D
ATT_W = DAQK_W + DAV_W + WAQ_W + WAKV_W
ATT_DAV, ATT_WAQ, ATT_WAK = DAQK_W, DAQK_W + DAV_W, DAQK_W + DAV_W + WAQ_W
ATT_WAV = ATT_WAK + WA_KV * WA_D
Y_DA, Y_WA = DN_W, DN_W + DAV_W

N_G, EPG = 4, 4
N_E = N_G * EPG
FF = 512
CAP = 128
ROUNDS = [TILES * P // CAP, SEQ // CAP]
ROWS = ROUNDS[0] * N_E * CAP
NEG = -1e30

OUT_TILES = [TILES, LAT_TILES]
F_ORDER = [2, 3, 0, 1]
B_ORDER = [3, 2, 1, 0]
STEPS = len(F_ORDER)
UNITS = 2 * DN_H
LEVELS = 7

F32 = mybir.dt.float32
U8, U32, I32 = mybir.dt.uint8, mybir.dt.uint32, mybir.dt.int32
ACT = mybir.ActivationFunctionType
AX = mybir.AxisListType

T_ID, T_LE, T_GE, T_LT, T_GT, T_ONE, T_NEG0, T_NEG1 = (i * P for i in range(8))
T_SEL = 8 * P
T_ROPE = T_SEL + 2 * P
ROPE_N = 4 * LAT_TILES * (DA_QK // 4) + 4 * LAT_TILES * (WA_D // 4)
T_EIDX = T_ROPE + ROPE_N
T_COLS = T_EIDX + 2 * N_E


def tables():
    p, f = np.arange(P)[:, None], np.arange(P)[None, :]
    t = np.zeros((P, T_COLS), np.float32)
    for at, m in ((T_ID, p == f), (T_LE, p <= f), (T_GE, p >= f), (T_LT, p < f), (T_GT, p > f), (T_ONE, p >= 0)):
        t[:, at:at + P] = m
    t[:, T_NEG0:T_NEG0 + P] = np.where(f <= p, 0.0, NEG)
    t[:, T_NEG1:T_NEG1 + P] = np.where(f >= p, 0.0, NEG)
    for r in range(2):
        t[:, T_SEL + r * P:T_SEL + (r + 1) * P] = p == r
    tok = np.arange(SEQ)
    at = T_ROPE
    for dim in (DA_QK, WA_D):
        nf = dim // 4
        inv = np.float32(ROPE_BASE) ** (-np.arange(nf, dtype=np.float32) / np.float32(nf))
        row, col = (tok // GRID_W).astype(np.float32), (tok % GRID_W).astype(np.float32)
        ang = np.stack([row[:, None] * inv, col[:, None] * inv], axis=1).astype(np.float32)
        for fn in (np.cos, np.sin):
            v = fn(ang).astype(np.float32).reshape(LAT_TILES, P, 2 * nf)
            t[:, at:at + LAT_TILES * 2 * nf] = v.transpose(1, 0, 2).reshape(P, -1)
            at += LAT_TILES * 2 * nf
    t[:, T_EIDX:T_EIDX + N_E] = N_E - np.arange(N_E)
    t[:, T_EIDX + N_E:T_EIDX + 2 * N_E] = CAP * np.arange(N_E)
    lev = np.zeros((P, 2, LEVELS, P), np.float32)
    for n in range(LEVELS):
        b = 1 << n
        lev[:, 0, n] = (p // b % 2 == 0) & (f // b == p // b + 1)
        lev[:, 1, n] = (p // b % 2 == 1) & (f // b == p // b - 1)
    return t, lev.reshape(P, -1)


class Stage:

    def __init__(self, sem, *per_layer):
        self.sem, self.per_layer, self.name = sem, per_layer, sem.name

    def at(self, layer, item):
        assert 0 <= item < self.per_layer[layer], (item, self.per_layer)
        return self.sem, sum(self.per_layer[:layer]) + item + 1

    def all(self, layer):
        return self.sem, sum(self.per_layer[:layer + 1])


class Banks:

    def __init__(self, psum):
        self.psum, self.n, self.owner, self.where = psum, 0, {}, {}

    def take(self, pe, copied, layer, item):
        b = self.n % 8
        self.n += 1
        if b in self.owner:
            pe.wait_ge(*self.owner[b])
        self.owner[b] = copied.at(layer, item)
        self.where[copied.name, layer, item] = b
        return self.psum[:, b, :]

    def of(self, copied, layer, item):
        return self.psum[:, self.where[copied.name, layer, item], :]


def runs(units):
    out = []
    for d in range(2):
        us = [u for u in units if u // DN_H == d]
        if us:
            out.append((d, us[0], len(us)))
    return out


def backbone(nc, io, out):
    ctx = ExitStack()

    def sb(name, shape, dt=F32):
        return ctx.enter_context(nc.sbuf_tensor(name, shape, dt))

    def sem(name):
        return ctx.enter_context(nc.semaphore(name))

    x = sb("x", [P, TILES, D])
    tab = sb("tab", [P, T_COLS])
    lev = sb("lev", [P, 2, LEVELS, P], U8)
    colsA = sb("colsA", [P, 48])
    ccol = sb("ccol", [P, KD, 2])
    convT = sb("convT", [P, DEPTH, TAPS * QKV_CH])
    smalls = {}
    sizes = [("alog", 2 * DN_H), ("dtb", 2 * DN_H), ("dng", DN_D), ("lam", 4 * DA_QK), ("subg", DA_V),
             ("sink", WA_H), ("rb", N_G + N_E)]
    small = sb("small", [P, DEPTH, sum(n for _, n in sizes)])
    at = 0
    for name, n in sizes:
        smalls[name] = slice(at, at + n)
        at += n

    def sm(layer, name):
        return small[:, layer, smalls[name]]

    rw = sb("rw", [P, DEPTH, KD, N_G + N_E])
    modT = sb("modT", [P, 4, KD, 2])
    normA = sb("normA", [P, 2, KD, 2])
    g2row = sb("g2row", [2, D])
    gateb = sb("gateb", [P, 2, D])
    stat = sb("stat", [P, 64])
    xstat = sb("xstat", [P, 3, 2, TILES])
    ring = sb("ring", [P, 3, 8 * 512])
    ARENA = 28416
    arena = sb("arena", [P, ARENA])

    def carve(at, *shape):
        n = int(np.prod(shape))
        assert at + n <= ARENA
        v = arena[:, at:at + n]
        if len(shape) > 1:
            names = "abcd"[:len(shape)]
            v = v.rearrange(f"p ({' '.join(names)}) -> p {' '.join(names)}", **dict(zip(names[1:], shape[1:])))
        return v

    R_B = 4096
    R_G = R_B + TILES * 9 * P
    R_Z = R_G + TILES * GAB_W
    rowsA = carve(0, P)[0:48, :]
    rowsC = carve(P, DEPTH, P)[0:TAPS * QKV_CH]
    lev_in = carve((1 + DEPTH) * P, 2 * LEVELS * P)
    hT = carve(0, KD, TILES * P)
    ycat = carve(0, TILES, D)
    qkv = carve(R_B, TILES, 3 * DN_W)
    yT = carve(R_B, KD, TILES * P)
    gab = carve(R_G, TILES, GAB_W)
    adarow = carve(R_Z, 6 * D)
    adab = carve(R_Z + 6 * D, 6 * D)
    xs = carve(R_Z + 12 * D, TILES, D)
    zat = carve(R_Z, TILES, ATT_W)
    at = R_Z + TILES * ATT_W
    daT = carve(at, 4, TILES * P); at += 4 * TILES * P
    waT = carve(at, 4, TILES * P); at += 4 * TILES * P
    ebuf = carve(at, 2, 2, 512); at += 2048
    pT = carve(at, 2, 4, P); at += 1024
    ropet = carve(at, 4, 256); at += 1024
    cpad = carve(at, 2, 2, SEQ + TAPS - 1); at += 4 * (SEQ + TAPS - 1)
    conv = carve(at, 2, TILES * P); at += 1024
    silu_c = carve(at, 2, TILES * P); at += 1024
    sq = carve(at - 2048, 2, 12 * DN_D)
    zeros = carve(ARENA - D, D)
    at = R_Z
    qT = carve(at, 3, TILES * P); at += 3 * TILES * P
    kT = carve(at, 3, TILES * P); at += 3 * TILES * P
    U_N = UNITS * P
    dn_bufs = []
    for _ in range(6):
        dn_bufs.append(carve(at, UNITS, P)); at += U_N
    b_A, b_D, b_nD, b_B, b_attT, b_Y0 = dn_bufs
    b_g, b_Y1 = (ring[:, 0, i * U_N:(i + 1) * U_N].rearrange("p (u n) -> p u n", u=UNITS) for i in range(2))
    b_Y = (b_Y0, b_Y1)
    vb = carve(at, UNITS, DN_D); at += UNITS * DN_D
    kbg = carve(at, UNITS, DN_D); at += UNITS * DN_D
    kdec = carve(at, UNITS, DN_D); at += UNITS * DN_D
    qdec = carve(at, UNITS, DN_D); at += UNITS * DN_D
    qdT = carve(at, 6, P); at += 6 * P
    nWT = carve(at, 6, P); at += 6 * P
    vnew = carve(at, UNITS, DN_D); at += UNITS * DN_D
    S = carve(at, 6, DN_D); at += 6 * DN_D
    dnu = sb("dnu", [P, 4, TILES, 4 * DN_H])
    dng = sb("dng", [P, TILES, UNITS])
    dnb = sb("dnb", [P, TILES, UNITS])
    dnx = sb("dnx", [P, 3, TILES, UNITS])
    dnc = sb("dnc", [P, 2, TILES, UNITS])
    egl = sb("egl", [P, TILES, 6])
    nalog = sb("nalog", [P, DEPTH, 2 * DN_H])
    gsub = sb("gsub", [P, DEPTH, DA_V])
    lamv = sb("lamv", [P, DEPTH, 8])
    lamt = sb("lamt", [P, DEPTH, 2, DA_QK])
    nsink = sb("nsink", [P, DEPTH, WA_H])
    hst = sb("hst", [P, 3, TILES, 12])
    ast = sb("ast", [P, 2, 8])
    moe_ring = carve(0, 3, 8 * 512)
    M_A = 3 * 4096
    h2T = carve(M_A, KD, TILES * P)
    hgT = carve(M_A, 2, KD, P)
    hid = carve(M_A + 2048, 2, FF)
    hidT = carve(M_A + 3072, 2, 4, P)
    yab = carve(M_A, 2, 2, D)
    h2tok = carve(M_A + 4096, TILES, D)
    hg = carve(M_A + 8192, 2, D)
    yb = carve(M_A + 10240, 2, D)
    xs2 = h2tok
    fin_g = carve(0, D)
    fin_x = carve(D, 2, D)
    lg = sb("lg", [P, TILES, N_G + N_E])
    rt = sb("rt", [P, 6, TILES, N_E])
    rs = sb("rs", [P, 12, TILES])
    posf = sb("posf", [P, TILES, 2])
    pos = sb("pos", [P, 2, TILES], U32)
    gates = sb("gates", [P, 2, TILES])
    cmax = sb("cmax", [P, 1])
    cmaxi = sb("cmaxi", [P, 1], I32)

    psum = ctx.enter_context(nc.psum_tensor("psum", [P, 8, 512], F32))
    banks = Banks(psum)
    hs = nc.dram_tensor("expert_in", (ROWS, D), F32, kind="Internal").ap()
    ys = nc.dram_tensor("expert_out", (ROWS, D), F32, kind="Internal").ap()

    ident, le, ge, lt, gt, ones = (tab[:, a:a + P] for a in (T_ID, T_LE, T_GE, T_LT, T_GT, T_ONE))
    r0 = T_ROPE
    cosB, sinB = (tab[:, r0 + i * 32:r0 + (i + 1) * 32].rearrange("p (t a f) -> p t a f", t=2, a=2) for i in range(2))
    r0 += 64
    cosW, sinW = (tab[:, r0 + i * 64:r0 + (i + 1) * 64].rearrange("p (t a f) -> p t a f", t=2, a=2) for i in range(2))

    def col_chunk(w, layer, *cols):
        return [(w[layer, :, a:b].rearrange("(k p) n -> p k n", p=P), o, b - a) for a, b, o in cols]

    ADA_CH, IN_CH, OUT_CH = 12, 7, 2
    CH = ADA_CH + IN_CH + OUT_CH
    IN_W = [DN_W, DN_W, DN_W, GAB_W, DAQK_W, DAV_W + WAKV_W, WAQ_W]

    def layer_chunks(layer):
        w = [col_chunk(io["ada_w"], layer, (512 * c, 512 * c + 512, 0)) for c in range(ADA_CH)]
        w += [col_chunk(io["w_in"], layer, (DN_W * c, DN_W * (c + 1), 0)) for c in range(3)]
        w.append(col_chunk(io["w_in"], layer, (COL_GATE, COL_ATT, 0)))
        w.append(col_chunk(io["w_in"], layer, (COL_ATT, COL_ATT + DAQK_W, 0)))
        w.append(col_chunk(io["w_in"], layer, (COL_ATT + ATT_DAV, COL_ATT + ATT_WAQ, 0),
                           (COL_ATT + ATT_WAK, COL_ATT + ATT_W, DAV_W)))
        w.append(col_chunk(io["w_in"], layer, (COL_ATT + ATT_WAQ, COL_ATT + ATT_WAK, 0)))
        w += [col_chunk(io["w_out"], layer, (512 * c, 512 * c + 512, 0)) for c in range(OUT_CH)]
        return w

    widths = [512] * ADA_CH + IN_W + [512] * OUT_CH
    SLOT_E = 16 * N_E // 2
    slot_total = {}
    run = [0, 0, 0]
    for layer in range(DEPTH):
        for c, parts in enumerate(layer_chunks(layer)):
            run[c % 3] += 16 * len(parts)
            slot_total[layer, c] = run[c % 3]
        for s in range(3):
            slot_total[layer, "experts", s] = run[s]
            run[s] += SLOT_E

    def chunk(c):
        return ring[:, c % 3, 0:8 * widths[c]].rearrange("p (k n) -> p k n", k=8)

    slot_in = [sem(f"slot_in{s}") for s in range(6)]
    const_in = sem("const_in")
    small_in = sem("small_in")
    x_in = sem("x_in")
    adab_in = sem("adab_in")
    zero_in = sem("zero_in")
    ZERO_N = N_E * CAP // P
    out_done = sem("out_done")
    dve_order, act_order, pool_order = sem("dve_order"), sem("act_order"), sem("pool_order")

    def st(name, *n):
        return Stage(sem(name), *(n if len(n) > 1 else n * 2))

    cols_psum, cols_copied = st("cols_psum", 3, 0), st("cols_copied", 5, 0)
    consts_made = st("consts_made", 1, 0)
    ada_psum, ada_copied = st("ada_psum", ADA_CH), st("ada_copied", ADA_CH)
    mod_psum, mod_copied = st("mod_psum", 1), st("mod_copied", 1)
    GB = [4, 2]
    gate_row_psum, gate_row_copied = (st(n, *(2 * k for k in GB)) for n in ("gate_row_psum", "gate_row_copied"))
    NORM_T = [TILES + n for n in OUT_TILES]
    ssq, rstd_done = st("ssq", NORM_T[0], NORM_T[1] + LAT_TILES), st("rstd_done", 2, 3)
    xs_ready = st("xs_ready", *NORM_T)
    hT_psum, hT_copied = st("hT_psum", 2 * KD), st("hT_copied", 2 * KD)
    qkv_psum, qkv_padded = st("qkv_psum", QKV_CH), st("qkv_padded", QKV_CH)
    conv_done, conv_silu = st("conv_done", QKV_CH), st("conv_silu", QKV_CH)
    qkvt_psum, qkvt_copied = st("qkvt_psum", QKV_CH), st("qkvt_copied", QKV_CH)
    z_psum, z_copied = st("z_psum", 4 * TILES, 4 * TILES - 2), st("z_copied", 4 * TILES, 4 * TILES - 2)
    roped = st("roped", 2 * LAT_TILES)
    att_psum, att_copied = st("att_psum", 8), st("att_copied", 8)
    DA_N, WA_N = [DA_H * n for n in OUT_TILES], [WA_H * n for n in OUT_TILES]
    da_s_psum, da_max, da_exp = st("da_s_psum", *(2 * n for n in DA_N)), st("da_max", *(2 * n for n in DA_N)), \
        st("da_exp", *(2 * n for n in DA_N))
    da_p = st("da_p", *DA_N)
    wa_s_psum, wa_max, wa_exp = (st(n, *WA_N) for n in ("wa_s_psum", "wa_max", "wa_exp"))
    AT_N = [a + b for a, b in zip(DA_N, WA_N)]
    pT_psum, pT_copied, o_psum = (st(n, *AT_N) for n in ("pT_psum", "pT_copied", "o_psum"))
    da_o, wa_o = st("da_o", *DA_N), st("wa_o", *WA_N)
    lam_sum = st("lam_sum", 1, 0)
    head_sq, head_ss = st("head_sq", *NORM_T), st("head_ss", *NORM_T)
    qk_norm = st("qk_norm", TILES)
    qk_rs, qk_scale, beta_ready = (st(n, 1) for n in ("qk_rs", "qk_scale", "beta_ready"))
    sp_arg, sp_exp, g_ready, cum_psum, cum_exp, coef = (st(n, 1) for n in
                                                       ("sp_arg", "sp_exp", "g_ready", "cum_psum", "cum_exp", "coef"))
    qkT_psum, qkT_copied = st("qkT_psum", 6), st("qkT_copied", 6)
    def steps(name, n=1):
        return st(name, STEPS * n)

    def out_steps(name, n):
        return st(name, STEPS * n, (STEPS - 2) * n)
    gmask, dec_psum, dec_exp, dec_ready = steps("gmask"), steps("dec_psum", 3), steps("dec_exp", 3), steps("dec_ready")
    dn_prod, y_init = steps("dn_prod"), steps("y_init")
    kk_psum, a_made = steps("kk_psum", 4), steps("a_made", 4)
    qk_psum, att_made = out_steps("qk_psum", 4), out_steps("att_made", 4)
    bt_psum, bt_copied = steps("bt_psum", 3), steps("bt_copied", 3)
    at_psum, at_copied = out_steps("at_psum", 3), out_steps("at_copied", 3)
    qd_psum, qd_copied = out_steps("qd_psum", 2), out_steps("qd_copied", 2)
    NL = LEVELS - 1
    y_merged = steps("y_merged", 3 * LEVELS)
    PSUM_AT, COPY_AT = {"p": -2, "y": -1, "x": 0}, {"p": -1, "x": 0}
    inv_psum, inv_copied = steps("inv_psum", 9 * NL), steps("inv_copied", 6 * NL)

    def inv(kind, j, lv, g):
        return (j * 3 * NL + 3 * lv + PSUM_AT[kind]) * 3 + g

    def invc(kind, j, lv, g):
        return (j * 2 * NL + 2 * lv + COPY_AT[kind]) * 3 + g

    w_psum, w_copied = steps("w_psum", 2), steps("w_copied", 2)
    v_psum, v_copied = steps("v_psum", 2), steps("v_copied", 2)
    so_psum, so_copied = out_steps("so_psum", 2), out_steps("so_copied", 2)
    s_psum, s_scaled, s_ready = steps("s_psum"), steps("s_scaled"), steps("s_ready")
    hn_mul, y_done = (st(n, *OUT_TILES) for n in ("hn_mul", "y_done"))
    hn_rs, s_cleared = st("hn_rs", 1), st("s_cleared", 1)
    yT_psum, yT_copied = st("yT_psum", KD), st("yT_copied", KD)
    wo_psum, wo_scaled = (st(n, *(2 * k for k in OUT_TILES)) for n in ("wo_psum", "wo_scaled"))
    x_mid = st("x_mid", *(2 * k for k in OUT_TILES))
    lg_psum, lg_copied, rt_exp, asg, rank_psum, pos_ready = (st(n, 1) for n in (
        "lg_psum", "lg_copied", "rt_exp", "asg", "rank_psum", "pos_ready"))
    rt_exp2, cmax_ready = st("rt_exp2", 1), st("cmax_ready", 1)
    rank_copied = st("rank_copied", 1)
    h2tok_psum, h2tok_copied = (st(n, *(2 * k for k in OUT_TILES)) for n in ("h2tok_psum", "h2tok_copied"))
    scattered = sem("scattered")
    experts_done = st("experts_done", 1)
    gathered = [sem(f"gathered{i}") for i in range(2)]
    comb_a, x_next = st("comb_a", *OUT_TILES), st("x_next", *OUT_TILES)
    fin_ready = st("fin_ready", LAT_TILES, 0)
    fin_in = sem("fin_in")

    class Experts:

        def __init__(self):
            self.in_ = [sem(f"hg_in{i}") for i in range(2)]
            self.out = [sem(f"y_out{i}") for i in range(2)]
            self.hgT_psum, self.hgT_copied = sem("hgT_psum"), sem("hgT_copied")
            self.gate_psum, self.gate_silu = sem("gate_psum"), sem("gate_silu")
            self.up_psum, self.hid_made = sem("up_psum"), sem("hid_made")
            self.hidT_psum, self.hidT_copied = sem("hidT_psum"), sem("hidT_copied")
            self.down_psum, self.y_low, self.y_high = sem("down_psum"), sem("y_low"), sem("y_high")

    fast = Experts()

    class Serial:

        def __init__(self, layer):
            self.pe = sem(f"more_pe{layer}")
            self.act = sem(f"more_act{layer}")
            self.dve = sem(f"more_dve{layer}")
            self.loads, self.out = sem(f"more_in{layer}"), sem(f"more_out{layer}")
            self.cleared, self.scat = (sem(f"more_{n}{layer}") for n in ("cleared", "scat"))

    more = [Serial(l) for l in range(DEPTH)]
    SMALL_N = 16 * (10 * DEPTH + 1)
    eps_col = stat[:, 0:1]

    def gathered_by(layer, t):
        return 32 * (sum(OUT_TILES[:layer]) // 2 + t // 2 + 1)


    groups = [list(range(4 * g, 4 * g + 4)) for g in range(3)]
    halves_of = [slice(DN_H * d + r, DN_H * d + DN_H, 2) for d in range(2) for r in range(2)]
    LAST_HALF = [1, 3, 3]

    def tile_of(j, u):
        return F_ORDER[j] if u < DN_H else B_ORDER[j]

    def pair(u):
        return (u // DN_H) * 3 + (u % DN_H) // 2

    def tok(t):
        return slice(t * P, (t + 1) * P)

    def wants_out(layer, j):
        return layer < DEPTH - 1 or j >= 2

    def keys_of(t):
        return list(range(TILES)) if t < LAT_TILES else [2, 3]

    def seqs(layer, ch):
        return 1 if layer == DEPTH - 1 and ch < 3 else 2

    def z_jobs(layer):
        jobs = []
        for c in range(3, IN_CH):
            for t in range(TILES):
                lean = layer == DEPTH - 1 and t >= LAT_TILES
                if c == 3:
                    a = DN_W if lean else 0
                    jobs.append((c, t, [(a, GAB_W, gab[:, t, a:GAB_W])]))
                elif c == 4:
                    a = DAQK_W // 2 if lean else 0
                    jobs.append((c, t, [(a, DAQK_W, zat[:, t, a:DAQK_W])]))
                elif c == 5:
                    jobs.append((c, t, [(0, DAV_W, zat[:, t, ATT_DAV:ATT_WAQ]),
                                        (DAV_W, DAV_W + WAKV_W, zat[:, t, ATT_WAK:ATT_W])]))
                elif not lean:
                    jobs.append((c, t, [(0, WAQ_W, zat[:, t, ATT_WAQ:ATT_WAK])]))
        return jobs

    def z_done(layer, c, t):
        return z_copied.at(layer, [j[:2] for j in z_jobs(layer)].index((c, t)))

    def all_z(eng, layer):
        eng.wait_ge(*z_copied.all(layer))

    def da_units(layer):
        return [(t, h) for t in range(OUT_TILES[layer]) for h in range(DA_H)]

    def wa_units(layer):
        return [(t, h) for t in range(OUT_TILES[layer]) for h in range(WA_H)]

    def dn_i(layer, j, per, g, only_wanted):
        return per * (j - (2 if only_wanted and layer == DEPTH - 1 else 0)) + g

    block = ctx.enter_context(nc.Block())

    @block.tensor
    def _(pe):
        mm, T = pe.matmul, pe.transpose

        def need_chunk(layer, c):
            pe.wait_ge(slot_in[c % 3], slot_total[layer, c])

        pe.wait_ge(const_in, 16 * (5 + DEPTH))
        b = banks.take(pe, cols_copied, 0, 0)
        T(b[:, 0:48], rowsA[:, :], ident[0:48, 0:48]).then_inc(cols_psum.sem, 1)
        for l in range(DEPTH):
            b = banks.take(pe, cols_copied, 0, 1 + l)
            T(b[:, 0:45], rowsC[:, l, :], ident[0:45, 0:45]).then_inc(cols_psum.sem, 1)

        def modulation(layer):
            if layer == 0:
                pe.wait_ge(*cols_copied.at(0, 3))
            for c in range(ADA_CH):
                need_chunk(layer, c)
                b = banks.take(pe, ada_copied, layer, c)
                for k in range(KD):
                    m = mm(b[0:2, :], ccol[:, k, :], chunk(c)[:, k, :], start=k == 0, stop=k == KD - 1)
                m.then_inc(ada_psum.sem, 1)
            b = banks.take(pe, mod_copied, layer, 0)
            pe.wait_ge(*ada_copied.at(layer, ADA_CH - 1))
            for n, part in enumerate((0, 1, 3, 4)):
                for k in range(KD):
                    o = (n * KD + k) * 2
                    m = T(b[:, o:o + 2], adarow[0:2, part * D + k * P:part * D + (k + 1) * P], ident[0:2, 0:2])
            m.then_inc(mod_psum.sem, 1)
            gate_rows(layer, adarow[0:2, 2 * D:3 * D], 0)

        def gate_rows(layer, row, item0):
            for i in range(GB[layer]):
                b = banks.take(pe, gate_row_copied, layer, item0 + i)
                mm(b[:, :], tab[0:2, T_SEL + (i // 2) * P:T_SEL + (i // 2 + 1) * P],
                   row[:, (i % 2) * 512:(i % 2 + 1) * 512], start=True, stop=True)\
                    .then_inc(gate_row_psum.sem, 1)

        def turn(layer, n_tiles, src, ready, filled, copied, item0=0):
            for k in range(KD):
                b = banks.take(pe, copied, layer, item0 + k)
                for t in range(n_tiles):
                    if k == 0:
                        pe.wait_ge(*ready(t))
                    m = T(b[:, tok(t)], src(t)[:, k * P:(k + 1) * P], ident)
                m.then_inc(filled.sem, 1)

        def projection(layer):
            pe.wait_ge(*hT_copied.at(layer, KD - 1))
            jobs = z_jobs(layer)
            n = 0
            for c in range(IN_CH):
                cc = ADA_CH + c
                need_chunk(layer, cc)
                if c < 3:
                    for s in range(3):
                        ch = 3 * c + s
                        w = SEQ * seqs(layer, ch)
                        b = banks.take(pe, qkv_padded, layer, ch)
                        for k in range(KD):
                            m = mm(b[:, 0:w], chunk(cc)[:, k, s * P:(s + 1) * P], hT[:, k, 0:w],
                                   start=k == 0, stop=k == KD - 1)
                        m.then_inc(qkv_psum.sem, 1)
                        if ch >= 2:
                            turn_conv(layer, ch - 2)
                else:
                    while n < len(jobs) and jobs[n][0] == c:
                        _, t, parts = jobs[n]
                        a, e = parts[0][0], parts[-1][1]
                        b = banks.take(pe, z_copied, layer, n)
                        for k in range(KD):
                            m = mm(b[:, 0:e - a], hT[:, k, tok(t)], chunk(cc)[:, k, a:e],
                                   start=k == 0, stop=k == KD - 1)
                        m.then_inc(z_psum.sem, 1)
                        n += 1
                if c == 3:
                    turn_conv(layer, QKV_CH - 2)
                    turn_conv(layer, QKV_CH - 1)

        def turn_conv(layer, ch):
            pe.wait_ge(*conv_silu.at(layer, ch))
            b = banks.take(pe, qkvt_copied, layer, ch)
            for t in range(2 * seqs(layer, ch)):
                m = T(b[:, tok(t)], silu_c[:, ch % 2, tok(t)], ident)
            m.then_inc(qkvt_psum.sem, 1)

        def attention(layer):
            nt = OUT_TILES[layer]
            pe.wait_ge(*roped.all(layer))
            all_z(pe, layer)
            for i in range(8):
                b = banks.take(pe, att_copied, layer, i)
                is_k = i in (2, 3, 7)
                for t in range(TILES if is_k else nt):
                    if i < 4:
                        src = zat[:, t, i * P:(i + 1) * P]
                    elif i < 7:
                        src = zat[:, t, ATT_WAQ + (i - 4) * P:ATT_WAQ + (i - 3) * P]
                    else:
                        src = zat[:, t, ATT_WAK:ATT_WAV]
                    m = T(b[:, tok(t)], src, ident)
                m.then_inc(att_psum.sem, 1)
            pe.wait_ge(*att_copied.all(layer))
            da, wa = da_units(layer), wa_units(layer)

            def scores(n):
                if n < len(da):
                    t, h = da[n]
                    k0, k1 = keys_of(t)[0] * P, TILES * P
                    for a in range(2):
                        hh = 2 * h + a
                        p0 = DA_QK * (hh % 4)
                        b = banks.take(pe, da_exp, layer, 2 * n + a)
                        mm(b[:, 0:k1 - k0], daT[p0:p0 + DA_QK, hh // 4, tok(t)], daT[p0:p0 + DA_QK, 2 + hh // 4, k0:k1],
                           start=True, stop=True).then_inc(da_s_psum.sem, 1)
                elif n < len(da) + len(wa):
                    t, h = wa[n - len(da)]
                    k0, k1 = keys_of(t)[0] * P, TILES * P
                    p0 = WA_D * (h // 3)
                    b = banks.take(pe, wa_exp, layer, n - len(da))
                    mm(b[:, 0:k1 - k0], waT[p0:p0 + WA_D, h % 3, tok(t)], waT[p0:p0 + WA_D, 3, k0:k1],
                       start=True, stop=True).then_inc(wa_s_psum.sem, 1)

            def turn_weights(n):
                is_da = n < len(da)
                keys = keys_of((da + wa)[n][0])
                pe.wait_ge(*(da_p.at(layer, n) if is_da else wa_exp.at(layer, n - len(da))))
                b = banks.take(pe, pT_copied, layer, n)
                for i in range(len(keys)):
                    m = T(b[:, tok(i)], ebuf[:, n % 2, 0, tok(i)], ident)
                m.then_inc(pT_psum.sem, 1)

            def values(n):
                is_da = n < len(da)
                t, h = da[n] if is_da else wa[n - len(da)]
                keys = keys_of(t)
                pe.wait_ge(*pT_copied.at(layer, n))
                b = banks.take(pe, *((da_o, layer, n) if is_da else (wa_o, layer, n - len(da))))
                v0 = ATT_DAV + h * DA_V if is_da else ATT_WAV + (h // 3) * WA_D
                for i, kt in enumerate(keys):
                    m = mm(b[:, 0:64], pT[:, n % 2, i, :], zat[:, kt, v0:v0 + 64], start=i == 0, stop=i == len(keys) - 1)
                m.then_inc(o_psum.sem, 1)

            N = len(da) + len(wa)
            scores(0)
            scores(1)
            turn_weights(0)
            for n in range(N):
                scores(n + 2)
                if n + 1 < N:
                    turn_weights(n + 1)
                values(n)

        def deltanet(layer):
            nt = OUT_TILES[layer]
            pe.wait_ge(*g_ready.at(layer, 0))
            b = banks.take(pe, cum_exp, layer, 0)
            cum = b[:, 0:3 * TILES * UNITS].rearrange("p (s t u) -> p s t u", s=3, t=TILES)
            for s, d, m in ((0, 0, le), (0, 1, ge), (1, 0, gt), (1, 1, lt)):
                us = slice(d * DN_H, (d + 1) * DN_H)
                mm(cum[:, s, :, us], m, dng[:, :, us], start=True, stop=True)
            mm(cum[:, 2], ones, dng[:, :, :], start=True, stop=True).then_inc(cum_psum.sem, 1)
            pe.wait_ge(*qk_norm.all(layer))
            for i in range(6):
                b = banks.take(pe, qkT_copied, layer, i)
                for t in range(TILES if i >= 3 else nt):
                    m = T(b[:, tok(t)], qkv[:, t, i * P:(i + 1) * P], ident)
                m.then_inc(qkT_psum.sem, 1)
            pe.wait_ge(*qkT_copied.all(layer))
            decays(layer, 0)
            for j in range(STEPS):
                step(layer, j)
            state_w(layer, STEPS - 1)
            state_v(layer, STEPS - 1)
            state_os(layer, STEPS - 1)

        def decays(layer, j):
            pe.wait_ge(*gmask.at(layer, j))
            for g, us in enumerate(groups):
                b = banks.take(pe, dec_exp, layer, 3 * j + g)
                for d, u0, n in runs(us):
                    m = mm(b[:, (u0 - us[0]) * P:(u0 - us[0] + n) * P], le if d == 0 else ge,
                           b_g[:, u0:u0 + n, :], start=True, stop=True)
                m.then_inc(dec_psum.sem, 1)

        def step(layer, j):
            want = wants_out(layer, j)
            Y = b_Y[j % 2]
            for lhs, filled, made in ((kT, kk_psum, a_made), (qT, qk_psum, att_made)):
                if lhs is qT and not want:
                    continue
                for g, us in enumerate(halves_of):
                    b = banks.take(pe, made, layer, dn_i(layer, j, 4, g, lhs is qT))
                    for i, u in enumerate(range(UNITS)[us]):
                        h, t, p0 = u % DN_H, tile_of(j, u), 64 * (u % 2)
                        m = mm(b[:, i * P:(i + 1) * P], lhs[p0:p0 + 64, h // 2, tok(t)], kT[p0:p0 + 64, h // 2, tok(t)],
                               start=True, stop=True)
                    m.then_inc(filled.sem, 1)
            if j > 0:
                state_w(layer, j - 1)
            for g, us in enumerate(groups):
                pe.wait_ge(*a_made.at(layer, 4 * j + LAST_HALF[g]))
                b = banks.take(pe, bt_copied, layer, 3 * j + g)
                for i, u in enumerate(us):
                    m = T(b[:, i * P:(i + 1) * P], b_A[:, u, :], ident)
                m.then_inc(bt_psum.sem, 1)
            if j > 0:
                state_v(layer, j - 1)
            for lv in range(NL + 1):
                if lv > 0:
                    for g, us in enumerate(groups):
                        pe.wait_ge(*inv_copied.at(layer, invc("x", j, lv - 1, g)))
                        b = banks.take(pe, inv_copied, layer, invc("p", j, lv, g))
                        for i, u in enumerate(us):
                            m = mm(b[:, i * P:(i + 1) * P], b_B[:, u, :], b_A[:, u, :], start=True, stop=True)
                        m.then_inc(inv_psum.sem, 1)
                    for g, us in enumerate(groups):
                        pe.wait_ge(*inv_copied.at(layer, invc("p", j, lv, g)))
                        b = banks.take(pe, y_merged, layer, (j * LEVELS + lv) * 3 + g)
                        for i, u in enumerate(us):
                            m = mm(b[:, i * P:(i + 1) * P], b_nD[:, u, :], Y[:, u, :], start=True, stop=True)
                        m.then_inc(inv_psum.sem, 1)
                if lv < NL:
                    for g, us in enumerate(groups):
                        pe.wait_ge(*y_merged.at(layer, (j * LEVELS + lv) * 3 + g))
                        b = banks.take(pe, inv_copied, layer, invc("x", j, lv, g))
                        for i, u in enumerate(us):
                            m = T(b[:, i * P:(i + 1) * P], Y[:, u, :], ident)
                        m.then_inc(inv_psum.sem, 1)
                if lv == 0 and j > 0:
                    state_os(layer, j - 1)
                if lv == 1 and want:
                    turn_attention(layer, j)
                if lv == 2 and j + 1 < STEPS:
                    decays(layer, j + 1)
                if lv == 3 and want:
                    turn_queries(layer, j)

        def turn_attention(layer, j):
            for g, us in enumerate(groups):
                pe.wait_ge(*att_made.at(layer, dn_i(layer, j, 4, LAST_HALF[g], True)))
                b = banks.take(pe, at_copied, layer, dn_i(layer, j, 3, g, True))
                for i, u in enumerate(us):
                    m = T(b[:, i * P:(i + 1) * P], b_D[:, u, :], ident)
                m.then_inc(at_psum.sem, 1)

        def turn_queries(layer, j):
            pe.wait_ge(*dn_prod.at(layer, j))
            for g, (p0, p1) in enumerate(((0, 4), (4, 6))):
                b = banks.take(pe, qd_copied, layer, dn_i(layer, j, 2, g, True))
                for q in range(p0, p1):
                    m = T(b[:, (q - p0) * P:(q - p0 + 1) * P], qdec[:, 2 * q:2 * q + 2, :], ident)
                m.then_inc(qd_psum.sem, 1)

        def state_w(layer, j):
            pe.wait_ge(*y_merged.at(layer, (j * LEVELS + NL) * 3 + 2))
            pe.wait_ge(*dn_prod.at(layer, j))
            for g, (p0, p1) in enumerate(((0, 4), (4, 6))):
                b = banks.take(pe, w_copied, layer, 2 * j + g)
                for u in range(2 * p0, 2 * p1):
                    q, r = pair(u) - p0, 64 * (u % 2)
                    m = mm(b[r:r + 64, q * P:(q + 1) * P], kbg[:, u, :], b_Y[j % 2][:, u, :], start=True, stop=True)
                m.then_inc(w_psum.sem, 1)

        def state_v(layer, j):
            pe.wait_ge(*w_copied.at(layer, 2 * j + 1))
            if j > 0:
                pe.wait_ge(*s_ready.at(layer, j - 1))
            else:
                pe.wait_ge(*s_cleared.at(layer, 0))
            for g in range(2):
                b = banks.take(pe, v_copied, layer, 2 * j + g)
                for i, u in enumerate(range(g, UNITS, 2)):
                    o, r = b[:, i * 64:(i + 1) * 64], 64 * (u % 2)
                    mm(o, b_Y[j % 2][:, u, :], vb[:, u, :], start=True, stop=False)
                    m = mm(o, nWT[r:r + 64, pair(u), :], S[r:r + 64, pair(u), :], start=False, stop=True)
                m.then_inc(v_psum.sem, 1)

        def state_os(layer, j):
            pe.wait_ge(*v_copied.at(layer, 2 * j + 1))
            if wants_out(layer, j):
                pe.wait_ge(*qd_copied.at(layer, dn_i(layer, j, 2, 1, True)))
                pe.wait_ge(*at_copied.at(layer, dn_i(layer, j, 3, 2, True)))
                for g in range(2):
                    b = banks.take(pe, so_copied, layer, dn_i(layer, j, 2, g, True))
                    for i, u in enumerate(range(g, UNITS, 2)):
                        o, r = b[:, i * 64:(i + 1) * 64], 64 * (u % 2)
                        mm(o, qdT[r:r + 64, pair(u), :], S[r:r + 64, pair(u), :], start=True, stop=False)
                        m = mm(o, b_attT[:, u, :], vnew[:, u, :], start=False, stop=True)
                    m.then_inc(so_psum.sem, 1)
            b = banks.take(pe, s_ready, layer, j)
            for u in range(UNITS):
                r, q = 64 * (u % 2), pair(u)
                m = mm(b[r:r + 64, q * 64:(q + 1) * 64], kdec[:, u, :], vnew[:, u, :], start=True, stop=True)
            m.then_inc(s_psum.sem, 1)

        def output(layer):
            nt = OUT_TILES[layer]
            pe.wait_ge(*wa_o.all(layer))
            turn(layer, nt, lambda t: ycat[:, t, :], lambda t: y_done.at(layer, t), yT_psum, yT_copied)
            pe.wait_ge(*yT_copied.all(layer))
            n = 0
            for c in range(OUT_CH):
                cc = ADA_CH + IN_CH + c
                need_chunk(layer, cc)
                for t in range(nt):
                    b = banks.take(pe, wo_scaled, layer, n)
                    for k in range(KD):
                        m = mm(b[:, :], yT[:, k, tok(t)], chunk(cc)[:, k, :], start=k == 0, stop=k == KD - 1)
                    m.then_inc(wo_psum.sem, 1)
                    n += 1
            gate2(layer)

        def gate2(layer):
            pe.wait_ge(*x_mid.all(layer))
            gate_rows(layer, g2row[0:2, :], GB[layer])

        def router(layer):
            nt = OUT_TILES[layer]
            turn(layer, nt, lambda t: xs2[:, t, :], lambda t: xs_ready.at(layer, TILES + t),
                 hT_psum, hT_copied, KD)
            pe.wait_ge(*hT_copied.all(layer))
            b = banks.take(pe, lg_copied, layer, 0)
            for t in range(nt):
                for k in range(KD):
                    m = mm(b[:, t * 20:(t + 1) * 20], h2T[:, k, tok(t)], rw[:, layer, k, :], start=k == 0, stop=k == KD - 1)
            m.then_inc(lg_psum.sem, 1)
            for t in range(nt):
                for half in range(2):
                    b = banks.take(pe, h2tok_copied, layer, 2 * t + half)
                    for q in range(4):
                        m = T(b[:, q * P:(q + 1) * P], h2T[:, 4 * half + q, tok(t)], ident)
                    m.then_inc(h2tok_psum.sem, 1)
            pe.wait_ge(*asg.at(layer, 0))
            b = banks.take(pe, rank_copied, layer, 0)
            for t in range(nt):
                for s in range(t):
                    mm(b[:, t * N_E:(t + 1) * N_E], ones, rt[:, 5, s, :], start=s == 0, stop=False)
                mm(b[:, t * N_E:(t + 1) * N_E], lt, rt[:, 5, t, :], start=t == 0, stop=True)
            for t in range(nt):
                m = mm(b[:, TILES * N_E:(TILES + 1) * N_E], ones, rt[:, 5, t, :], start=t == 0, stop=t == nt - 1)
            m.then_inc(rank_psum.sem, 1)

        def experts(layer):
            base = layer * N_E
            for b in range(8):
                if b in banks.owner:
                    pe.wait_ge(*banks.owner[b])

            def turn_in(filled, par):
                for half in range(2):
                    for q in range(4):
                        m = T(psum[:, half, q * P:(q + 1) * P], hg[:, par, (4 * half + q) * P:(4 * half + q + 1) * P], ident)
                m.then_inc(filled, 1)

            def product(dst, w, par, filled):
                for k in range(KD):
                    m = mm(dst, hgT[:, par, k, :], w[:, k, :], start=k == 0, stop=k == KD - 1)
                if filled is not None:
                    m.then_inc(filled, 1)

            def turn_hid(filled, par):
                for k in range(4):
                    m = T(psum[:, 4, k * P:(k + 1) * P], hid[:, par, k * P:(k + 1) * P], ident)
                m.then_inc(filled, 1)

            def down(filled, w, par):
                for half in range(2):
                    for k in range(4):
                        m = mm(psum[:, 5 + half, :], hidT[:, par, k, :], w[:, k, half * 512:(half + 1) * 512],
                               start=k == 0, stop=k == 3)
                    if filled is not None:
                        m.then_inc(filled, 1)
                return m

            def slot(par, q, k):
                r = ring if par == 0 else moe_ring
                return r[:, q, :].rearrange("p (k n) -> p k n", k=k)

            def landed(par, e):
                return [(slot_total[layer, "experts", q] if par == 0 else layer * SLOT_E) + 16 * (e + 1) for q in range(3)]

            def first(e, half, par):
                w = landed(par, half)
                pe.wait_ge(fast.in_[par], 16 * (half + 1) + layer * SLOT_E)
                if not (layer == 0 and isinstance(e, int) and e == 0):
                    pe.wait_ge(fast.hgT_copied, base + e)
                turn_in(fast.hgT_psum, par)
                if not (layer == 0 and isinstance(e, int) and e == 0):
                    pe.wait_ge(fast.gate_silu, base + e)
                pe.wait_ge(fast.hgT_copied, base + e + 1)
                pe.wait_ge(slot_in[3 * par], w[0])
                product(psum[:, 2, :], slot(par, 0, 8), par, fast.gate_psum)

            def second(e, half, par):
                w = landed(par, half)
                pe.wait_ge(slot_in[3 * par + 1], w[1])
                product(psum[:, 3, :], slot(par, 1, 8), par, fast.up_psum)

            def third(e, half, par):
                w = landed(par, half)
                pe.wait_ge(slot_in[3 * par + 2], w[2])
                pe.wait_ge(fast.hidT_copied, base + e + 1)
                down(fast.down_psum, slot(par, 2, 4), par)

            def both(e, half, par):
                first(e, half, par)
                pe.wait_ge(fast.hid_made, base + e)
                turn_hid(fast.hidT_psum, 1 - par)
                second(e, half, par)
                if not (layer == 0 and isinstance(e, int)):
                    pe.wait_ge(fast.y_low, base + e - 1)
                    pe.wait_ge(fast.y_high, base + e - 1)
                third(e - 1, half - 1 if par == 0 else half, 1 - par)

            first(0, 0, 0)
            second(0, 0, 0)
            both(1, 0, 1)
            with pe.Fori(1, N_E // 2) as i:
                both(2 * i, i, 0)
                both(2 * i + 1, i, 1)
            pe.wait_ge(fast.hid_made, base + N_E)
            turn_hid(fast.hidT_psum, 1)
            pe.wait_ge(fast.y_low, base + N_E - 1)
            pe.wait_ge(fast.y_high, base + N_E - 1)
            third(N_E - 1, N_E // 2 - 1, 1)
            pe.wait_ge(fast.y_low, base + N_E)
            pe.wait_ge(fast.y_high, base + N_E)

            pe.wait_ge(*cmax_ready.at(layer, 0))
            most = pe.value_load(cmaxi[0:1, 0:1])
            sy = more[layer]
            with pe.If(most > CAP):
                pe.nop().then_inc(sy.pe, 1)
                with pe.Fori(0, (ROUNDS[layer] - 1) * N_E) as n:
                    pe.wait_ge(sy.loads, 64 * (n + 1))
                    turn_in(sy.pe, 0)
                    pe.wait_ge(sy.dve, 3 * n + 1)
                    product(psum[:, 2, :], slot(0, 0, 8), 0, None)
                    product(psum[:, 3, :], slot(0, 1, 8), 0, sy.pe)
                    pe.wait_ge(sy.dve, 3 * n + 2)
                    turn_hid(sy.pe, 0)
                    pe.wait_ge(sy.act, 3 * n + 2)
                    down(None, slot(0, 2, 4), 0).then_inc(sy.pe, 1)
                pe.wait_ge(sy.act, 3 * (ROUNDS[layer] - 1) * N_E)
                pe.wait_ge(sy.dve, 3 * (ROUNDS[layer] - 1) * N_E)
            banks.owner.clear()

        for layer in range(DEPTH):
            modulation(layer)
            turn(layer, TILES, lambda t: xs[:, t, :], lambda t: xs_ready.at(layer, t), hT_psum, hT_copied)
            projection(layer)
            attention(layer)
            deltanet(layer)
            output(layer)
            router(layer)
            experts(layer)

    @block.sync
    def _(sp):
        def weights_free(layer, c):
            if c < ADA_CH:
                sp.wait_ge(*ada_psum.at(layer, c))
            elif c < ADA_CH + 3:
                sp.wait_ge(*qkv_psum.at(layer, 3 * (c - ADA_CH) + 2))
            elif c < ADA_CH + IN_CH:
                last = max(n for n, j in enumerate(z_jobs(layer)) if j[0] == c - ADA_CH)
                sp.wait_ge(*z_psum.at(layer, last))
            else:
                sp.wait_ge(*wo_psum.at(layer, OUT_TILES[layer] * (c - ADA_CH - IN_CH + 1) - 1))

        sp.dma_start(tab[:, :], io["tables"]).then_inc(const_in, 16)
        sp.dma_start(rowsA[0:8, :], io["c"].rearrange("b (k p) -> (b k) p", p=P)).then_inc(const_in, 16)
        sp.dma_start(rowsA[8:16, :], io["c_ctx"].rearrange("(k p) -> k p", p=P)).then_inc(const_in, 16)
        sp.dma_start(rowsA[16:32, :], io["norm1_g"].rearrange("l (k p) -> (l k) p", p=P)).then_inc(const_in, 16)
        sp.dma_start(rowsA[32:48, :], io["norm2_g"].rearrange("l (k p) -> (l k) p", p=P)).then_inc(const_in, 16)
        for l in range(DEPTH):
            sp.dma_start(rowsC[:, l, :], io["dn_conv_w"][l].rearrange("j (c p) -> (j c) p", p=P)).then_inc(const_in, 16)

        for layer in range(DEPTH):
            if layer > 0:
                sp.wait_ge(*x_next.all(layer - 1))
            sp.dma_start(adab[0:2, :], io["ada_b"][layer].partition_broadcast(2)).then_inc(adab_in, 16)
            zeroed = 0
            for c, parts in enumerate(layer_chunks(layer)):
                if c >= 3:
                    weights_free(layer, c - 3)
                elif layer > 0:
                    sp.wait_ge(*((fast.gate_psum, layer * N_E - 1), (fast.up_psum, layer * N_E - 1),
                                 (fast.down_psum, 2 * (layer * N_E - 1)))[c])
                for src, o, n in parts:
                    sp.dma_start(chunk(c)[:, :, o:o + n], src).then_inc(slot_in[c % 3], 16)
                if layer == 0 and c == 2:
                    for t in range(TILES):
                        src = io["x"][0, tok(t), :] if t < LAT_TILES else io["ctx"][0, tok(t - LAT_TILES), :]
                        sp.dma_start(x[:, t, :], src).then_inc(x_in, 16)
                if layer == 0 and 3 <= c < ADA_CH:
                    if c == 3:
                        sp.wait_ge(*consts_made.at(0, 0))
                    while zeroed < ZERO_N * (c - 2) // (ADA_CH - 3):
                        sp.dma_start(hs[zeroed * P:(zeroed + 1) * P, :], zeros).then_inc(zero_in, 16)
                        zeroed += 1

            base = layer * N_E
            names = ("exp_w_gate", "exp_w_up", "exp_w_down")

            def load(q, e, par):
                k = 4 if q == 2 else 8
                dst = (ring if par == 0 else moe_ring)[:, q, :].rearrange("p (k n) -> p k n", k=k)
                src = io[names[q]][layer][bass.ds(e, 1)].rearrange("o (k p) n -> p (o k) n", p=P)
                return sp.dma_start(dst, src)

            for q in range(3):
                weights_free(layer, CH - 3 + q)
                if q == 0:
                    sp.wait_ge(*v_psum.at(layer, 2 * STEPS - 1))
                load(q, 0, 0).then_inc(slot_in[q], 16)
            sp.wait_ge(*wo_scaled.all(layer))
            sp.wait_ge(*x_mid.all(layer))
            for q in range(3):
                load(q, 1, 1).then_inc(slot_in[3 + q], 16)
            sp.wait_ge(scattered, 16 * 2 * sum(OUT_TILES[:layer + 1]))
            for par in range(2):
                sp.dma_start(hg[:, par, :], hs[par * CAP:(par + 1) * CAP, :]).then_inc(fast.in_[par], 16)

            def tick(e, par, loads=True, down=True, store=True):
                row_in, row_out, e1, e2 = (e + 2) * CAP, (e - 1) * CAP, e + 1, e + 2
                now, before, down_before = base + e + 1, base + e, 2 * (base + e)
                if not isinstance(e, int):
                    row_in, row_out, e1, e2, now, before, down_before = (
                        sp.snap(v) for v in (row_in, row_out, e1, e2, now, before, down_before))
                if loads:
                    sp.wait_ge(fast.hgT_psum, now)
                    sp.dma_start(hg[:, par, :], hs[bass.ds(row_in, CAP), :]).then_inc(fast.in_[par], 16)
                    sp.wait_ge(fast.gate_psum, now)
                    load(0, e2, par).then_inc(slot_in[3 * par], 16)
                    sp.wait_ge(fast.up_psum, now)
                    load(1, e2, par).then_inc(slot_in[3 * par + 1], 16)
                if down:
                    sp.wait_ge(fast.down_psum, down_before)
                    load(2, e1, 1 - par).then_inc(slot_in[3 * (1 - par) + 2], 16)
                if store:
                    sp.wait_ge(fast.y_low, before)
                    sp.wait_ge(fast.y_high, before)
                    sp.dma_start(ys[bass.ds(row_out, CAP), :], yb[:, 1 - par, :]).then_inc(fast.out[1 - par], 16)

            tick(0, 0, down=False, store=False)
            with sp.Fori(0, N_E // 2 - 2) as i:
                tick(2 * i + 1, 1)
                tick(2 * i + 2, 0)
            tick(N_E - 3, 1)
            tick(N_E - 2, 0, loads=False)
            tick(N_E - 1, 1, loads=False, down=False)
            tick(N_E, 0, loads=False, down=False)
            for par in range(2):
                sp.wait_ge(fast.out[par], (layer + 1) * SLOT_E)

            sy = more[layer]
            sp.wait_ge(*cmax_ready.at(layer, 0))
            most = sp.value_load(cmaxi[0:1, 0:1])
            n_more = (ROUNDS[layer] - 1) * N_E
            with sp.If(most > CAP):
                sp.wait_ge(sy.cleared, 1)
                with sp.Fori(0, n_more) as n:
                    sp.dma_start(hs[bass.ds((n + N_E) * CAP, CAP), :], hg[:, 1, :]).then_inc(sy.out, 16)
                sp.wait_ge(sy.scat, 16 * 2 * OUT_TILES[layer])
                with sp.Fori(0, ROUNDS[layer] - 1) as r:
                    with sp.Fori(0, N_E) as e:
                        n = r * N_E + e
                        row, e_ = sp.snap((n + N_E) * CAP), sp.snap(e)
                        now, done, sent = sp.snap(4 * n + 1), sp.snap(3 * n + 3), sp.snap(16 * (n_more + n))
                        sp.wait_ge(sy.out, sent)
                        sp.wait_ge(sy.pe, now)
                        sp.dma_start(hg[:, 0, :], hs[bass.ds(row, CAP), :]).then_inc(sy.loads, 16)
                        for q in range(3):
                            load(q, e_, 0).then_inc(sy.loads, 16)
                        sp.wait_ge(sy.act, done)
                        sp.wait_ge(sy.dve, done)
                        sp.dma_start(ys[bass.ds(row, CAP), :], yb[:, 0, :]).then_inc(sy.out, 16)
                sp.wait_ge(sy.out, 32 * n_more)
            sp.nop().then_inc(experts_done.sem, 1)

        sp.wait_ge(*experts_done.at(DEPTH - 1, 0))
        sp.dma_start(fin_g, io["final_norm_g"].partition_broadcast(P)).then_inc(fin_in, 16)
        for t in range(LAT_TILES):
            sp.wait_ge(*fin_ready.at(0, t))
            sp.dma_start(out[0, tok(t), :], fin_x[:, t, :]).then_inc(out_done, 16)
        sp.wait_ge(out_done, 16 * LAT_TILES)

    @block.scalar
    def _(act):
        go = act.activation
        count = [0]

        def link(ins):
            count[0] += 1
            ins.then_inc(act_order, 1)
            act.wait_ge(act_order, count[0])

        for l in range(DEPTH):
            for name, src in (("alog", io["dn_a_log"][l].rearrange("a h -> (a h)")),
                              ("dtb", io["dn_dt_bias"][l].rearrange("a h -> (a h)")),
                              ("dng", io["dn_norm_g"][l]), ("lam", io["da_lambda"][l].rearrange("a h -> (a h)")),
                              ("subg", io["da_subln_g"][l]), ("sink", io["wa_sink"][l])):
                act.dma_start(sm(l, name), src.partition_broadcast(P)).then_inc(small_in, 16)
            act.dma_start(sm(l, "rb")[:, 0:N_G], io["router_group_b"][l].partition_broadcast(P)).then_inc(small_in, 16)
            act.dma_start(sm(l, "rb")[:, N_G:], io["router_expert_b"][l].partition_broadcast(P)).then_inc(small_in, 16)
            act.dma_start(rw[:, l, :, 0:N_G], io["router_group_w"][l].rearrange("(k p) n -> p k n", p=P)).then_inc(small_in, 16)
            act.dma_start(rw[:, l, :, N_G:], io["router_expert_w"][l].rearrange("(k p) n -> p k n", p=P)).then_inc(small_in, 16)
        act.dma_start(lev_in, io["levels"]).then_inc(small_in, 16)

        act.wait_ge(*cols_psum.at(0, 0))
        act.copy(colsA[:, :], banks.of(cols_copied, 0, 0)[:, 0:48]).then_inc(cols_copied.sem, 1)
        for l in range(DEPTH):
            act.wait_ge(*cols_psum.at(0, 1 + l))
            act.copy(convT[:, l, :], banks.of(cols_copied, 0, 1 + l)[:, 0:45]).then_inc(cols_copied.sem, 1)
        act.wait_ge(*cols_copied.at(0, 0))
        go(ccol[:, :, :].rearrange("p k r -> p r k"), colsA[:, 0:2 * KD].rearrange("p (r k) -> p r k", r=2),
           ACT.Silu).then_inc(cols_copied.sem, 1)
        act.wait_ge(small_in, SMALL_N)
        link(go(nalog[:, :, :], small[:, :, smalls["alog"]], ACT.Exp))
        act.mul(nalog[:, :, :], nalog[:, :, :], -1.0)
        act.mul(nsink[:, :, :], small[:, :, smalls["sink"]], -1.0)
        act.wait_ge(*lam_sum.at(0, 0))
        go(lamv[:, :, 2:4], lamv[:, :, 0:2], ACT.Exp).then_inc(cols_copied.sem, 1)

        def gate_copies(layer, item0):
            for i in range(GB[layer]):
                act.wait_ge(*gate_row_psum.at(layer, item0 + i))
                act.copy(gateb[:, i // 2, (i % 2) * 512:(i % 2 + 1) * 512], banks.of(gate_row_copied, layer, item0 + i))\
                    .then_inc(gate_row_copied.sem, 1)

        def rstd(layer, w, nt, last):
            act.wait_ge(*ssq.at(layer, last))
            link(go(xstat[:, 1, w, 0:nt], xstat[:, 0, w, 0:nt], ACT.Ln, bias=eps_col, scale=1.0 / D))
            go(xstat[:, 2, w, 0:nt], xstat[:, 1, w, 0:nt], ACT.Exp, scale=-0.5).then_inc(rstd_done.sem, 1)

        def norm1(layer):
            if layer == 0:
                act.wait_ge(x_in, 16 * TILES)
            else:
                act.wait_ge(*x_next.all(layer - 1))
            for t in range(TILES):
                go(xs[:, t, :], x[:, t, :], ACT.Square, accum_out=xstat[:, 0, 0, t:t + 1]).then_inc(ssq.sem, 1)
            rstd(layer, 0, TILES, TILES - 1)

        def projection(layer):
            for ch in range(QKV_CH):
                act.wait_ge(*qkv_psum.at(layer, ch))
                ns = seqs(layer, ch)
                if ch >= 2:
                    act.wait_ge(*conv_done.at(layer, ch - 2))
                act.copy(cpad[:, ch % 2, 0:ns, 2:2 + SEQ], banks.of(qkv_padded, layer, ch)[:, 0:ns * SEQ]
                         .rearrange("p (s n) -> p s n", s=ns)).then_inc(qkv_padded.sem, 1)
                act.wait_ge(*conv_done.at(layer, ch))
                if ch >= 2:
                    act.wait_ge(*qkvt_psum.at(layer, ch - 2))
                go(silu_c[:, ch % 2, 0:ns * SEQ], conv[:, ch % 2, 0:ns * SEQ], ACT.Silu).then_inc(conv_silu.sem, 1)
            for n, (c, t, parts) in enumerate(z_jobs(layer)):
                act.wait_ge(*z_psum.at(layer, n))
                b, a0 = banks.of(z_copied, layer, n), parts[0][0]
                if c == 3:
                    if a0 == 0:
                        go(gab[:, t, 0:DN_W], b[:, 0:DN_W], ACT.Silu)
                    act.copy(gab[:, t, DN_W:], b[:, DN_W - a0:GAB_W - a0]).then_inc(z_copied.sem, 1)
                else:
                    for i, (a, e, dst) in enumerate(parts):
                        src = b[:, a - a0:e - a0]
                        if c == 6:
                            dst = dst.rearrange("p (r g d) -> p g r d", g=WA_KV, d=WA_D)
                            src = src.rearrange("p (g r d) -> p g r d", g=WA_KV, d=WA_D)
                        ins = act.copy(dst, src)
                    ins.then_inc(z_copied.sem, 1)

        def dn_numbers(layer):
            act.wait_ge(*sp_arg.at(layer, 0))
            link(go(dnu[:, 3], dnu[:, 1], ACT.Exp))
            go(dnu[:, 3], dnu[:, 3], ACT.Ln, bias=1.0).then_inc(sp_exp.sem, 1)
            act.wait_ge(*g_ready.at(layer, 0))
            go(dnb[:, :, :], dnu[:, 0, :, UNITS:], ACT.Exp, scale=-1.0).then_inc(beta_ready.sem, 1)
            act.wait_ge(*head_ss.at(layer, TILES - 1))
            link(go(hst[:, 1], hst[:, 0], ACT.Ln, bias=eps_col))
            go(hst[:, 2], hst[:, 1], ACT.Exp, scale=-0.5).then_inc(qk_rs.sem, 1)

        def attention(layer):
            nt = OUT_TILES[layer]
            for i in range(8):
                act.wait_ge(*att_psum.at(layer, i))
                is_k = i in (2, 3, 7)
                w = (TILES if is_k else nt) * P
                dst = (daT if i < 4 else waT)[:, i % 4, 0:w]
                scale = 1.0 if is_k else (DA_QK if i < 4 else WA_D) ** -0.5
                act.mul(dst, banks.of(att_copied, layer, i)[:, 0:w], scale).then_inc(att_copied.sem, 1)
            da, wa = da_units(layer), wa_units(layer)
            N = len(da) + len(wa)

            def exps(n):
                if n >= 2:
                    act.wait_ge(*pT_psum.at(layer, n - 2))
                if n < len(da):
                    w = len(keys_of(da[n][0])) * P
                    for a in range(2):
                        act.wait_ge(*da_max.at(layer, 2 * n + a))
                        go(ebuf[:, n % 2, a, 0:w], banks.of(da_exp, layer, 2 * n + a)[:, 0:w], ACT.Exp,
                           bias=ast[:, n % 2, a:a + 1], accum_out=ast[:, n % 2, 2 + a:3 + a]).then_inc(da_exp.sem, 1)
                elif n < N:
                    m = n - len(da)
                    t, h = wa[m]
                    w = len(keys_of(t)) * P
                    act.wait_ge(*wa_max.at(layer, m))
                    go(ast[:, n % 2, 3:4], sm(layer, "sink")[:, h:h + 1], ACT.Exp, bias=ast[:, n % 2, 1:2])
                    go(ebuf[:, n % 2, 0, 0:w], banks.of(wa_exp, layer, m)[:, 0:w], ACT.Exp,
                       bias=ast[:, n % 2, 1:2], accum_out=ast[:, n % 2, 2:3]).then_inc(wa_exp.sem, 1)

            exps(0)
            exps(1)
            for n in range(N):
                w = len(keys_of((da + wa)[n][0])) * P
                act.wait_ge(*pT_psum.at(layer, n))
                if n >= 2:
                    act.wait_ge(*o_psum.at(layer, n - 2))
                act.copy(pT[:, n % 2].rearrange("p i q -> p (i q)")[:, 0:w], banks.of(pT_copied, layer, n)[:, 0:w])\
                    .then_inc(pT_copied.sem, 1)
                exps(n + 2)

        def copy_groups(layer, filled, i0, copied, c0, dst):
            for g, us in enumerate(groups):
                act.wait_ge(*filled.at(layer, i0 + g))
                act.copy(dst[:, us[0]:us[0] + 4, :].rearrange("p u n -> p (u n)"), banks.of(copied, layer, c0 + g))\
                    .then_inc(copied.sem, 1)

        def deltanet(layer):
            nt = OUT_TILES[layer]
            act.wait_ge(*cum_psum.at(layer, 0))
            go(dnx[:, :, :, :].rearrange("p s t u -> p (s t u)"), banks.of(cum_exp, layer, 0)[:, 0:3 * TILES * UNITS],
               ACT.Exp).then_inc(cum_exp.sem, 1)
            for i in range(6):
                w = (TILES if i >= 3 else nt) * P
                act.wait_ge(*qkT_psum.at(layer, i))
                act.wait_ge(*o_psum.all(layer))
                act.wait_ge(*wa_o.all(layer))
                act.copy((qT if i < 3 else kT)[:, i % 3, 0:w], banks.of(qkT_copied, layer, i)[:, 0:w]).then_inc(qkT_copied.sem, 1)

            def decay(j):
                for g, us in enumerate(groups):
                    act.wait_ge(*dec_psum.at(layer, 3 * j + g))
                    if j > 0 and wants_out(layer, j - 1):
                        act.wait_ge(*at_psum.at(layer, dn_i(layer, j - 1, 3, 2, True)))
                    if j > 0:
                        act.wait_ge(*dec_ready.at(layer, j - 1))
                    go(b_D[:, us[0]:us[0] + 4, :].rearrange("p u n -> p (u n)"), banks.of(dec_exp, layer, 3 * j + g),
                       ACT.Exp).then_inc(dec_exp.sem, 1)

            def copy_w(j):
                for g, (p0, p1) in enumerate(((0, 4), (4, 6))):
                    act.wait_ge(*w_psum.at(layer, 2 * j + g))
                    act.mul(nWT[:, p0:p1, :].rearrange("p u n -> p (u n)"), banks.of(w_copied, layer, 2 * j + g)[:, 0:(p1 - p0) * P],
                            -1.0).then_inc(w_copied.sem, 1)

            decay(0)
            for j in range(STEPS):
                want = wants_out(layer, j)
                if j > 0:
                    copy_w(j - 1)
                copy_groups(layer, bt_psum, 3 * j, bt_copied, 3 * j, b_B)
                for lv in range(NL + 1):
                    if lv > 0:
                        copy_groups(layer, inv_psum, inv("p", j, lv, 0), inv_copied, invc("p", j, lv, 0), b_nD)
                    if lv < NL:
                        copy_groups(layer, inv_psum, inv("x", j, lv, 0), inv_copied, invc("x", j, lv, 0), b_A)
                    if lv == 1 and want:
                        if j > 0 and wants_out(layer, j - 1):
                            act.wait_ge(*so_psum.at(layer, dn_i(layer, j - 1, 2, 1, True)))
                        i = dn_i(layer, j, 3, 0, True)
                        copy_groups(layer, at_psum, i, at_copied, i, b_attT)
                    if lv == 2 and j + 1 < STEPS:
                        decay(j + 1)
                    if lv == 3 and want:
                        for g, (p0, p1) in enumerate(((0, 4), (4, 6))):
                            i = dn_i(layer, j, 2, g, True)
                            act.wait_ge(*qd_psum.at(layer, i))
                            act.copy(qdT[:, p0:p1, :].rearrange("p u n -> p (u n)"), banks.of(qd_copied, layer, i)[:, 0:(p1 - p0) * P])\
                                .then_inc(qd_copied.sem, 1)
            copy_w(STEPS - 1)
            act.wait_ge(*head_ss.all(layer))
            link(go(hst[:, 1, 0:nt, 0:10], hst[:, 0, 0:nt, 0:10], ACT.Ln, bias=eps_col, scale=1.0 / DN_D))
            go(hst[:, 2, 0:nt, 0:10], hst[:, 1, 0:nt, 0:10], ACT.Exp, scale=-0.5).then_inc(hn_rs.sem, 1)

        def output(layer):
            nt = OUT_TILES[layer]
            for k in range(KD):
                act.wait_ge(*yT_psum.at(layer, k))
                act.copy(yT[:, k, 0:nt * P], banks.of(yT_copied, layer, k)[:, 0:nt * P]).then_inc(yT_copied.sem, 1)
            act.wait_ge(*x_mid.all(layer))
            gate_copies(layer, GB[layer])
            for t in range(nt):
                go(xs2[:, t, :], x[:, t, :], ACT.Square, accum_out=xstat[:, 0, 1, t:t + 1]).then_inc(ssq.sem, 1)
            rstd(layer, 1, nt, NORM_T[layer] - 1)

        def router(layer):
            nt = OUT_TILES[layer]
            for i in range(2 * nt):
                act.wait_ge(*h2tok_psum.at(layer, i))
                act.copy(h2tok[:, i // 2, (i % 2) * 512:(i % 2 + 1) * 512], banks.of(h2tok_copied, layer, i)).then_inc(h2tok_copied.sem, 1)
            act.wait_ge(*rt_exp.at(layer, 0))
            link(go(rt[:, 0, 0:nt, 0:4], rt[:, 0, 0:nt, 0:4], ACT.Exp))
            go(rs[:, 3, 0:nt], rs[:, 2, 0:nt], ACT.Exp).then_inc(rt_exp2.sem, 1)

        def experts(layer):
            base = layer * N_E

            def silu_gate(sy, now, par):
                act.wait_ge(sy.gate_psum, now)
                go(hid[:, par, :], psum[:, 2, :], ACT.Silu).then_inc(sy.gate_silu, 1)

            def low_half(sy, now, par, stored):
                act.wait_ge(sy.hidT_psum, now)
                act.copy(hidT[:, par].rearrange("p k n -> p (k n)"), psum[:, 4, :]).then_inc(sy.hidT_copied, 1)
                act.wait_ge(sy.down_psum, 2 * now - 1)
                if stored is not None:
                    act.wait_ge(sy.out[par], stored)
                act.copy(yb[:, par, 0:512], psum[:, 5, :]).then_inc(sy.y_low, 1)

            silu_gate(fast, base + 1, 0)
            for e in range(1, 3):
                silu_gate(fast, base + e + 1, e % 2)
                low_half(fast, base + e, 1 - e % 2, layer * SLOT_E if layer > 0 else None)
            with act.Fori(1, N_E // 2 - 1) as i:
                silu_gate(fast, base + 2 * i + 2, 1)
                low_half(fast, base + 2 * i + 1, 0, layer * SLOT_E + 16 * i)
                silu_gate(fast, base + 2 * i + 3, 0)
                low_half(fast, base + 2 * i + 2, 1, layer * SLOT_E + 16 * i)
            silu_gate(fast, base + N_E, 1)
            low_half(fast, base + N_E - 1, 0, (layer + 1) * SLOT_E - 16)
            low_half(fast, base + N_E, 1, (layer + 1) * SLOT_E - 16)

            act.wait_ge(*cmax_ready.at(layer, 0))
            most = act.value_load(cmaxi[0:1, 0:1])
            sy = more[layer]
            with act.If(most > CAP):
                with act.Fori(0, (ROUNDS[layer] - 1) * N_E) as n:
                    act.wait_ge(sy.pe, 4 * n + 3)
                    go(hid[:, 0, :], psum[:, 2, :], ACT.Silu).then_inc(sy.act, 1)
                    act.wait_ge(sy.pe, 4 * n + 4)
                    act.copy(hidT[:, 0].rearrange("p k n -> p (k n)"), psum[:, 4, :]).then_inc(sy.act, 1)
                    act.wait_ge(sy.pe, 4 * n + 5)
                    act.copy(yb[:, 0, 0:512], psum[:, 5, :]).then_inc(sy.act, 1)
            for t in range(OUT_TILES[layer]):
                act.wait_ge(gathered[t % 2], gathered_by(layer, t))
                act.mul(yab[:, t % 2, 0, :], yab[:, t % 2, 0, :], gates[:, 0, t:t + 1]).then_inc(comb_a.sem, 1)

        for layer in range(DEPTH):
            norm1(layer)
            gate_copies(layer, 0)
            projection(layer)
            dn_numbers(layer)
            attention(layer)
            deltanet(layer)
            output(layer)
            router(layer)
            experts(layer)

        act.wait_ge(*x_next.all(DEPTH - 1))
        for t in range(LAT_TILES):
            go(fin_x[:, t, :], x[:, t, :], ACT.Square, accum_out=xstat[:, 0, 0, t:t + 1]).then_inc(ssq.sem, 1)
        rstd(DEPTH - 1, 0, LAT_TILES, NORM_T[-1] + LAT_TILES - 1)

    @block.vector
    def _(dve):
        tt, ts, stt = dve.tensor_tensor, dve.tensor_scalar, dve.scalar_tensor_tensor
        count = [0]

        def link(ins):
            count[0] += 1
            ins.then_inc(dve_order, 1)
            dve.wait_ge(dve_order, count[0])

        def sum_of(o, i):
            return dve.tensor_reduce(o, i, AX.X, ALU.add)

        dve.memset(eps_col, EPS)
        dve.wait_ge(small_in, SMALL_N)
        link(dve.tensor_copy(lev[:, :, :, :].rearrange("p a b c -> p (a b c)"), lev_in))
        for l in range(DEPTH):
            v = sm(l, "lam").rearrange("p (a b n) -> p a b n", a=2, b=2)
            link(tt(lamt[:, l], v[:, :, 0, :], v[:, :, 1, :], ALU.mult))
            ins = sum_of(lamv[:, l, 0:2], lamt[:, l])
        ins.then_inc(lam_sum.sem, 1)
        dve.wait_ge(*cols_copied.at(0, 4))
        for l in range(DEPTH):
            lam_init = 0.8 - 0.6 * math.exp(-0.3 * l)
            link(tt(lamv[:, l, 4:5], lamv[:, l, 3:4], lamv[:, l, 2:3], ALU.subtract))
            link(ts(lamv[:, l, 5:6], lamv[:, l, 4:5], -lam_init, None, ALU.add))
            ts(gsub[:, l, :], sm(l, "subg"), 1.0 - lam_init, None, ALU.mult)

        def modulation(layer):
            dve.wait_ge(adab_in, 16 * (layer + 1))
            for c in range(ADA_CH):
                dve.wait_ge(*ada_psum.at(layer, c))
                dst = g2row[0:2, (c - 10) * 512:(c - 9) * 512] if c >= 10 else adarow[0:2, c * 512:(c + 1) * 512]
                tt(dst, banks.of(ada_copied, layer, c)[0:2, :], adab[0:2, c * 512:(c + 1) * 512], ALU.add).then_inc(ada_copied.sem, 1)
            dve.wait_ge(*mod_psum.at(layer, 0))
            dve.tensor_copy(modT[:, :, :, :].rearrange("p a k r -> p (a k r)"), banks.of(mod_copied, layer, 0)[:, 0:64])\
                .then_inc(mod_copied.sem, 1)
            dve.wait_ge(*mod_copied.at(layer, 0))
            if layer == 0:
                dve.wait_ge(*cols_copied.at(0, 0))
            for w in range(2):
                a = 16 + 16 * w + 8 * layer
                ins = stt(normA[:, w], modT[:, 2 * w + 1], 1.0, colsA[:, a:a + 8].unsqueeze(2).to_broadcast([P, KD, 2]),
                          ALU.add, ALU.mult)
            link(ins)

        def normed(layer, w, nt, dst, xsd):
            dve.wait_ge(*rstd_done.at(layer, w))
            for t in range(nt):
                ts(xsd[:, t, :], x[:, t, :], xstat[:, 2, w, t:t + 1], None, ALU.mult).then_inc(xs_ready.sem, 1)
            for k in range(KD):
                dve.wait_ge(*hT_psum.at(layer, w * KD + k))
                b = banks.of(hT_copied, layer, w * KD + k)
                for r in range(nt // 2):
                    ins = ts(dst[:, k, r * SEQ:(r + 1) * SEQ], b[:, r * SEQ:(r + 1) * SEQ], normA[:, w, k, r:r + 1],
                             modT[:, 2 * w, k, r:r + 1], ALU.mult, ALU.add)
                ins.then_inc(hT_copied.sem, 1)

        def projection(layer):
            def copy_turned(ch):
                dve.wait_ge(*qkvt_psum.at(layer, ch))
                n = 2 * seqs(layer, ch)
                dve.tensor_copy(qkv[:, 0:n, ch * P:(ch + 1) * P], banks.of(qkvt_copied, layer, ch)[:, 0:n * P]
                                .rearrange("p (t n) -> p t n", t=n)).then_inc(qkvt_copied.sem, 1)

            dve.memset(cpad[:, :, :, 0:TAPS // 2], 0.0)
            link(dve.memset(cpad[:, :, :, TAPS // 2 + SEQ:], 0.0))
            for ch in range(QKV_CH):
                dve.wait_ge(*qkv_padded.at(layer, ch))
                ns = seqs(layer, ch)
                if ch >= 2:
                    dve.wait_ge(*conv_silu.at(layer, ch - 2))
                acc = conv[:, ch % 2, 0:ns * SEQ].rearrange("p (s n) -> p s n", s=ns)
                for j in range(TAPS):
                    src = cpad[:, ch % 2, 0:ns, j:j + SEQ]
                    w = convT[:, layer, j * QKV_CH + ch:j * QKV_CH + ch + 1]
                    if j == 0:
                        link(ts(acc, src, w, None, ALU.mult))
                    elif j < TAPS - 1:
                        link(stt(acc, src, w, acc, ALU.mult, ALU.add))
                    else:
                        stt(acc, src, w, acc, ALU.mult, ALU.add).then_inc(conv_done.sem, 1)
                if ch >= 2:
                    copy_turned(ch - 2)
            copy_turned(QKV_CH - 2)
            copy_turned(QKV_CH - 1)

        def dn_numbers(layer):
            dve.wait_ge(*z_done(layer, 3, TILES - 1))
            u = dnu[:, 0]
            ab = gab[:, :, DN_W:]
            tt(u[:, :, 0:UNITS], ab[:, :, 0:UNITS], sm(layer, "dtb").unsqueeze(1).to_broadcast([P, TILES, UNITS]), ALU.add)
            link(ts(u[:, :, UNITS:], ab[:, :, UNITS:], -1.0, None, ALU.mult))
            link(ts(dnu[:, 1], u, -1.0, None, ALU.mult))
            link(tt(dnu[:, 1], u, dnu[:, 1], ALU.min))
            ts(dnu[:, 2], u, 0.0, None, ALU.max).then_inc(sp_arg.sem, 1)
            dve.wait_ge(*sp_exp.at(layer, 0))
            link(tt(dnu[:, 0], dnu[:, 2], dnu[:, 3], ALU.add))
            tt(dng[:, :, :], dnu[:, 0, :, 0:UNITS], nalog[:, layer, :].unsqueeze(1).to_broadcast([P, TILES, UNITS]),
               ALU.mult).then_inc(g_ready.sem, 1)
            for t in range(TILES):
                h0 = DN_H if layer == DEPTH - 1 and t >= LAT_TILES else 0
                dve.wait_ge(*head_sq.at(layer, t))
                sum_of(hst[:, 0, t, h0:2 * DN_H], sq[:, t % 2, h0 * DN_D:].rearrange("p (h d) -> p h d", d=DN_D)).then_inc(head_ss.sem, 1)
            dve.wait_ge(*qk_rs.at(layer, 0))
            ts(hst[:, 2, :, 0:DN_H], hst[:, 2, :, 0:DN_H], DN_D ** -0.5, None, ALU.mult).then_inc(qk_scale.sem, 1)

        def attention(layer):
            da, wa = da_units(layer), wa_units(layer)
            N = len(da) + len(wa)

            def maxes(n):
                if n < len(da):
                    w = len(keys_of(da[n][0])) * P
                    for a in range(2):
                        dve.wait_ge(*da_s_psum.at(layer, 2 * n + a))
                        dve.tensor_reduce(ast[:, n % 2, a:a + 1], banks.of(da_exp, layer, 2 * n + a)[:, 0:w], AX.X, ALU.max,
                                          negate=True).then_inc(da_max.sem, 1)
                elif n < N:
                    m = n - len(da)
                    t, h = wa[m]
                    w = len(keys_of(t)) * P
                    b = banks.of(wa_exp, layer, m)
                    dve.wait_ge(*wa_s_psum.at(layer, m))
                    if t < LAT_TILES:
                        o = tok(1 - t)
                        neg = tab[:, T_NEG0:T_NEG0 + P] if t == 0 else tab[:, T_NEG1:T_NEG1 + P]
                        link(tt(b[:, o], b[:, o], neg, ALU.add))
                    link(dve.tensor_reduce(ast[:, n % 2, 0:1], b[:, 0:w], AX.X, ALU.max, negate=True))
                    tt(ast[:, n % 2, 1:2], ast[:, n % 2, 0:1], nsink[:, layer, h:h + 1], ALU.min).then_inc(wa_max.sem, 1)

            def weights(n):
                s = ast[:, n % 2]
                if n < len(da):
                    w = len(keys_of(da[n][0])) * P
                    dve.wait_ge(*da_exp.at(layer, 2 * n + 1))
                    link(dve.reciprocal(s[:, 4:6], s[:, 2:4]))
                    link(tt(s[:, 5:6], s[:, 5:6], lamv[:, layer, 5:6], ALU.mult))
                    e0, e1 = ebuf[:, n % 2, 0, 0:w], ebuf[:, n % 2, 1, 0:w]
                    link(ts(e0, e0, s[:, 4:5], None, ALU.mult))
                    stt(e0, e1, s[:, 5:6], e0, ALU.mult, ALU.add).then_inc(da_p.sem, 1)
                else:
                    dve.wait_ge(*wa_exp.at(layer, n - len(da)))
                    if n - len(da) >= 2:
                        dve.wait_ge(*wa_o.at(layer, n - len(da) - 2))
                    link(tt(s[:, 4:5], s[:, 2:3], s[:, 3:4], ALU.add))
                    link(dve.reciprocal(s[:, 4:5], s[:, 4:5]))

            def result(n):
                dve.wait_ge(*o_psum.at(layer, n))
                if n < len(da):
                    t, h = da[n]
                    dve.tensor_copy(ycat[:, t, Y_DA + h * DA_V:Y_DA + (h + 1) * DA_V], banks.of(da_o, layer, n)[:, 0:64])\
                        .then_inc(da_o.sem, 1)
                else:
                    m = n - len(da)
                    t, h = wa[m]
                    ts(ycat[:, t, Y_WA + h * WA_D:Y_WA + (h + 1) * WA_D], banks.of(wa_o, layer, m)[:, 0:64],
                       ast[:, n % 2, 4:5], None, ALU.mult).then_inc(wa_o.sem, 1)

            maxes(0)
            maxes(1)
            weights(0)
            for n in range(N):
                maxes(n + 2)
                if n + 1 < N:
                    weights(n + 1)
                result(n)

        def deltanet(layer):
            nt = OUT_TILES[layer]
            dve.wait_ge(*cum_exp.at(layer, 0))
            dve.wait_ge(*beta_ready.at(layer, 0))
            ts(dnc[:, 0], dnb[:, :, :], -1.0, None, ALU.mult)
            tt(dnc[:, 1], dnb[:, :, :], dnx[:, 0], ALU.mult)
            for r in range(2):
                ins = dve.tensor_copy(egl[64 * r:64 * r + 64, :, :], dnx[64 * r:64 * r + 64, 2].rearrange("p t (q r) -> p t q r", r=2)[:, :, :, r])
            ins.then_inc(coef.sem, 1)

            def state(j):
                for g in range(2):
                    dve.wait_ge(*v_psum.at(layer, 2 * j + g))
                    dve.tensor_copy(vnew[:, g::2, :], banks.of(v_copied, layer, 2 * j + g)[:, 0:DN_W]
                                    .rearrange("p (u n) -> p u n", u=DN_H)).then_inc(v_copied.sem, 1)
                if wants_out(layer, j):
                    for g in range(2):
                        i = dn_i(layer, j, 2, g, True)
                        dve.wait_ge(*so_psum.at(layer, i))
                        b = banks.of(so_copied, layer, i)[:, 0:DN_W].rearrange("p (e a n) -> p e a n", e=2, n=DN_D)
                        for d in range(2):
                            dst = ycat[:, tile_of(j, d * DN_H), 0:DN_W].rearrange("p (a g n) -> p g a n", g=2, n=DN_D)[:, g]
                            src = b[:, d]
                            if j % 2 == 0:
                                ins = dve.tensor_copy(dst, src)
                            else:
                                ins = tt(dst, src, dst, ALU.add)
                        ins.then_inc(so_copied.sem, 1)
                dve.wait_ge(*s_psum.at(layer, j))
                dve.wait_ge(*s_scaled.at(layer, j))
                f = S[:, :, :].rearrange("p q n -> p (q n)")
                tt(f, banks.of(s_ready, layer, j)[:, 0:6 * DN_D], f, ALU.add).then_inc(s_ready.sem, 1)

            for j in range(STEPS):
                want = wants_out(layer, j)
                dve.wait_ge(*dec_ready.at(layer, j))
                three = lambda v: v[:, 0:3 * P].rearrange("p (u n) -> p u n", u=3)
                for g, us in enumerate(halves_of):
                    dve.wait_ge(*kk_psum.at(layer, 4 * j + g))
                    tt(b_A[:, us, :], three(banks.of(a_made, layer, 4 * j + g)), b_nD[:, us, :], ALU.mult).then_inc(a_made.sem, 1)
                if want:
                    for g, us in enumerate(halves_of):
                        i = dn_i(layer, j, 4, g, True)
                        dve.wait_ge(*qk_psum.at(layer, i))
                        tt(b_D[:, us, :], three(banks.of(att_made, layer, i)), b_D[:, us, :], ALU.mult).then_inc(att_made.sem, 1)
                dve.wait_ge(*y_init.at(layer, j))
                for lv in range(LEVELS):
                    for g, us in enumerate(groups):
                        if lv == 0:
                            dve.wait_ge(*bt_copied.at(layer, 3 * j + g))
                            dve.wait_ge(*a_made.at(layer, 4 * j + 3))
                        else:
                            dve.wait_ge(*inv_psum.at(layer, inv("y", j, lv, g)))
                            b = banks.of(y_merged, layer, (j * LEVELS + lv) * 3 + g)
                        for d, u0, n in runs(us):
                            m = lev[:, d, lv, :].unsqueeze(1).to_broadcast([P, n, P])
                            src = b_B[:, u0:u0 + n, :] if lv == 0 else \
                                b[:, (u0 - us[0]) * P:(u0 - us[0] + n) * P].rearrange("p (u n) -> p u n", u=n)
                            ins = dve.copy_predicated(b_Y[j % 2][:, u0:u0 + n, :], m, src)
                        ins.then_inc(y_merged.sem, 1)
                    if lv == 0 and j > 0:
                        state(j - 1)
            state(STEPS - 1)
            for t in range(nt):
                dve.wait_ge(*head_sq.at(layer, TILES + t))
                sum_of(hst[:, 0, t, 0:10], sq[:, t % 2, 0:640].rearrange("p (h d) -> p h d", d=64)).then_inc(head_ss.sem, 1)
            dve.wait_ge(*hn_rs.at(layer, 0))
            for t in range(nt):
                y = ycat[:, t, 0:640].rearrange("p (h d) -> p h d", d=64)
                tt(y, y, hst[:, 2, t, 0:10].unsqueeze(2).to_broadcast([P, 10, 64]), ALU.mult).then_inc(hn_mul.sem, 1)

        def output(layer):
            nt = OUT_TILES[layer]
            n = 0
            for c in range(OUT_CH):
                for t in range(nt):
                    dve.wait_ge(*wo_psum.at(layer, n))
                    dve.wait_ge(*gate_row_copied.at(layer, GB[layer] - 1))
                    dve.wait_ge(*yT_psum.at(layer, KD - 1))
                    if n >= 2:
                        dve.wait_ge(*x_mid.at(layer, n - 2))
                    tt(ycat[:, n % 2, 0:512], banks.of(wo_scaled, layer, n),
                       gateb[:, t // 2, c * 512:(c + 1) * 512], ALU.mult).then_inc(wo_scaled.sem, 1)
                    n += 1

        def router(layer):
            nt = OUT_TILES[layer]
            dve.wait_ge(*lg_psum.at(layer, 0))
            L = lg[:, 0:nt, :]
            tt(L, banks.of(lg_copied, layer, 0)[:, 0:nt * 20].rearrange("p (t n) -> p t n", n=20),
               sm(layer, "rb").unsqueeze(1).to_broadcast([P, nt, 20]), ALU.add).then_inc(lg_copied.sem, 1)
            dve.wait_ge(*lg_copied.at(layer, 0))
            R = lambda i: rs[:, i, 0:nt]
            key, oh1, oh2, lem, pv, as_ = (rt[:, i, 0:nt, :] for i in range(6))
            bc = lambda v, n: v.unsqueeze(2).to_broadcast([P, nt, n])
            eidx = lambda n: tab[:, T_EIDX:T_EIDX + n].unsqueeze(1).to_broadcast([P, nt, n])

            def first_max(values, n, o, mx, scr):
                link(dve.tensor_reduce(mx, values, AX.X, ALU.max))
                link(tt(scr, values, bc(mx, n), ALU.is_equal))
                link(tt(scr, scr, eidx(n), ALU.mult))
                link(dve.tensor_reduce(R(6), scr, AX.X, ALU.max))
                link(tt(o, scr, bc(R(6), n), ALU.is_equal))

            g_oh = oh1[:, :, 0:N_G]
            first_max(L[:, :, 0:N_G], N_G, g_oh, R(0), key[:, :, 0:N_G])
            link(ts(pv[:, :, 0:N_G], g_oh, -NEG, NEG, ALU.mult, ALU.add))
            for g in range(N_G):
                ins = tt(lem[:, :, g * EPG:(g + 1) * EPG], L[:, :, N_G + g * EPG:N_G + (g + 1) * EPG],
                         pv[:, :, g:g + 1].to_broadcast([P, nt, EPG]), ALU.add)
            link(ins)
            first_max(lem, N_E, oh1, R(1), key)
            link(ts(key, oh1, NEG, None, ALU.mult))
            link(tt(lem, lem, key, ALU.add))
            first_max(lem, N_E, oh2, R(4), key)
            link(tt(R(2), R(4), R(1), ALU.subtract))
            tt(as_, oh1, oh2, ALU.add).then_inc(asg.sem, 1)
            tt(key[:, :, 0:N_G], L[:, :, 0:N_G], bc(R(0), N_G), ALU.subtract).then_inc(rt_exp.sem, 1)
            dve.wait_ge(*rt_exp2.at(layer, 0))
            link(sum_of(R(5), key[:, :, 0:N_G]))
            link(ts(R(7), R(3), 1.0, None, ALU.add))
            link(tt(R(5), R(5), R(7), ALU.mult))
            link(dve.reciprocal(gates[:, 0, 0:nt], R(5)))
            tt(gates[:, 1, 0:nt], gates[:, 0, 0:nt], R(3), ALU.mult)
            dve.wait_ge(*rank_psum.at(layer, 0))
            b = banks.of(rank_copied, layer, 0)
            link(dve.tensor_reduce(cmax[:, :], b[:, TILES * N_E:(TILES + 1) * N_E], AX.X, ALU.max))
            link(dve.tensor_copy(cmaxi[:, :], cmax[:, :]))
            dve.tensor_copy(pv, b[:, 0:nt * N_E].rearrange("p (t n) -> p t n", n=N_E)).then_inc(rank_copied.sem, 1)
            dve.wait_ge(*rank_copied.at(layer, 0))
            dve.nop().then_inc(cmax_ready.sem, 1)
            link(tt(lem, pv, tab[:, T_EIDX + N_E:T_EIDX + 2 * N_E].unsqueeze(1).to_broadcast([P, nt, N_E]), ALU.add))
            for r in range(1, ROUNDS[layer]):
                link(ts(key, pv, float(r * CAP), float((N_E - 1) * CAP), ALU.is_ge, ALU.mult))
                link(tt(lem, lem, key, ALU.add))
            for i, o in enumerate((oh1, oh2)):
                link(tt(key, o, lem, ALU.mult))
                link(sum_of(posf[:, 0:nt, i], key))
                ins = dve.tensor_copy(pos[:, i, 0:nt], posf[:, 0:nt, i])
            ins.then_inc(pos_ready.sem, 1)

        def experts(layer):
            base = layer * N_E

            def turned_in(sy, now, par):
                dve.wait_ge(sy.hgT_psum, now)
                dve.tensor_copy(hgT[:, par].rearrange("p k n -> p (k n)"), psum[:, 0:2, :].rearrange("p b n -> p (b n)"))\
                    .then_inc(sy.hgT_copied, 1)

            def hidden(sy, now, par):
                dve.wait_ge(sy.gate_silu, now)
                dve.wait_ge(sy.up_psum, now)
                tt(hid[:, par, :], psum[:, 3, :], hid[:, par, :], ALU.mult).then_inc(sy.hid_made, 1)

            def high_half(sy, now, par, stored):
                dve.wait_ge(sy.down_psum, 2 * now)
                if stored is not None:
                    dve.wait_ge(sy.out[par], stored)
                dve.tensor_copy(yb[:, par, 512:1024], psum[:, 6, :]).then_inc(sy.y_high, 1)

            dve.wait_ge(*lg_psum.at(layer, 0))
            dve.wait_ge(*h2tok_psum.all(layer))
            turned_in(fast, base + 1, 0)
            hidden(fast, base + 1, 0)
            for e in range(1, 3):
                turned_in(fast, base + e + 1, e % 2)
                hidden(fast, base + e + 1, e % 2)
                high_half(fast, base + e, 1 - e % 2, layer * SLOT_E if layer > 0 else None)
            with dve.Fori(1, N_E // 2 - 1) as i:
                turned_in(fast, base + 2 * i + 2, 1)
                hidden(fast, base + 2 * i + 2, 1)
                high_half(fast, base + 2 * i + 1, 0, layer * SLOT_E + 16 * i)
                turned_in(fast, base + 2 * i + 3, 0)
                hidden(fast, base + 2 * i + 3, 0)
                high_half(fast, base + 2 * i + 2, 1, layer * SLOT_E + 16 * i)
            turned_in(fast, base + N_E, 1)
            hidden(fast, base + N_E, 1)
            high_half(fast, base + N_E - 1, 0, (layer + 1) * SLOT_E - 16)
            high_half(fast, base + N_E, 1, (layer + 1) * SLOT_E - 16)

            dve.wait_ge(*cmax_ready.at(layer, 0))
            most = dve.value_load(cmaxi[0:1, 0:1])
            sy = more[layer]
            with dve.If(most > CAP):
                with dve.Fori(0, (ROUNDS[layer] - 1) * N_E) as n:
                    dve.wait_ge(sy.pe, 4 * n + 2)
                    dve.tensor_copy(hgT[:, 0].rearrange("p k n -> p (k n)"), psum[:, 0:2, :].rearrange("p b n -> p (b n)"))\
                        .then_inc(sy.dve, 1)
                    dve.wait_ge(sy.act, 3 * n + 1)
                    tt(hid[:, 0, :], psum[:, 3, :], hid[:, 0, :], ALU.mult).then_inc(sy.dve, 1)
                    dve.wait_ge(sy.pe, 4 * n + 5)
                    dve.tensor_copy(yb[:, 0, 512:1024], psum[:, 6, :]).then_inc(sy.dve, 1)
            dve.wait_ge(*gate_row_copied.all(layer))
            for t in range(OUT_TILES[layer]):
                dve.wait_ge(*comb_a.at(layer, t))
                a, b = yab[:, t % 2, 0, :], yab[:, t % 2, 1, :]
                link(stt(b, b, gates[:, 1, t:t + 1], a, ALU.mult, ALU.add))
                link(tt(b, b, gateb[:, t // 2, :], ALU.mult))
                tt(x[:, t, :], x[:, t, :], b, ALU.add).then_inc(x_next.sem, 1)

        for layer in range(DEPTH):
            modulation(layer)
            normed(layer, 0, TILES, hT, xs)
            projection(layer)
            dn_numbers(layer)
            attention(layer)
            deltanet(layer)
            output(layer)
            normed(layer, 1, OUT_TILES[layer], h2T, xs2)
            router(layer)
            experts(layer)
        dve.wait_ge(*rstd_done.at(DEPTH - 1, 2))
        dve.wait_ge(fin_in, 16)
        for t in range(LAT_TILES):
            stt(fin_x[:, t, :], x[:, t, :], xstat[:, 2, 0, t:t + 1], fin_g, ALU.mult, ALU.mult).then_inc(fin_ready.sem, 1)

    @block.gpsimd
    def _(pool):
        tt = pool.tensor_tensor
        count = [0]

        def link(ins):
            count[0] += 1
            ins.then_inc(pool_order, 1)
            pool.wait_ge(pool_order, count[0])

        pool.memset(zeros, 0.0).then_inc(consts_made.sem, 1)

        def ropes(layer):
            for t in range(LAT_TILES):
                for c0, n, cos, sin, need in ((0, 4 * DA_H, cosB, sinB, (4,)), (ATT_WAQ, WA_H + WA_KV, cosW, sinW, (5, 6))):
                    for c in need:
                        pool.wait_ge(*z_done(layer, c, t))
                    d = DA_QK if c0 == 0 else WA_D
                    v = zat[:, t, c0:c0 + n * d].rearrange("p (h a b f) -> p h a b f", h=n, a=2, b=2)
                    tmp = [ropet[:, i, :].rearrange("p (h a f) -> p h a f", h=n, a=2) for i in range(4)]
                    for a in range(2):
                        x1, x2 = v[:, :, a, 0, :], v[:, :, a, 1, :]
                        cc, ss = (m[:, t, a, :].unsqueeze(1).to_broadcast([P, n, d // 4]) for m in (cos, sin))
                        q = [m[:, :, a, :] for m in tmp]
                        tt(q[0], x1, cc, ALU.mult)
                        tt(q[1], x2, ss, ALU.mult)
                        tt(q[2], x2, cc, ALU.mult)
                        link(tt(q[3], x1, ss, ALU.mult))
                        tt(x1, q[0], q[1], ALU.subtract)
                        ins = tt(x2, q[2], q[3], ALU.add)
                        if a == 0:
                            link(ins)
                    ins.then_inc(roped.sem, 1)
                    pool.wait_ge(*roped.at(layer, 2 * t + (c0 > 0)))

        def qk_norms(layer):
            for t in range(TILES):
                c0 = DN_W if layer == DEPTH - 1 and t >= LAT_TILES else 0
                pool.wait_ge(*qkvt_copied.all(layer))
                if t >= 2:
                    pool.wait_ge(*head_ss.at(layer, t - 2))
                tt(sq[:, t % 2, c0:], qkv[:, t, c0:2 * DN_W], qkv[:, t, c0:2 * DN_W], ALU.mult).then_inc(head_sq.sem, 1)
            pool.wait_ge(*qk_scale.at(layer, 0))
            for t in range(TILES):
                h0 = DN_H if layer == DEPTH - 1 and t >= LAT_TILES else 0
                v = qkv[:, t, h0 * DN_D:2 * DN_W].rearrange("p (h d) -> p h d", d=DN_D)
                tt(v, v, hst[:, 2, t, h0:].unsqueeze(2).to_broadcast([P, 2 * DN_H - h0, DN_D]), ALU.mult).then_inc(qk_norm.sem, 1)

        def deltanet(layer):
            nt = OUT_TILES[layer]
            pool.wait_ge(*coef.at(layer, 0))
            pool.wait_ge(*qk_norm.all(layer))
            pool.wait_ge(*wa_o.all(layer))
            if layer == 0:
                pool.wait_ge(zero_in, 16 * ZERO_N)
            pool.memset(S[:, :, :], 0.0).then_inc(s_cleared.sem, 1)
            pool.wait_ge(*s_cleared.at(layer, 0))
            pool.wait_ge(*z_psum.all(layer))
            if layer > 0:
                pool.wait_ge(*ada_psum.at(layer, 0))

            def both(op):
                for d in range(2):
                    ins = op(d, slice(d * DN_H, (d + 1) * DN_H))
                return ins

            def tile(j, d):
                return (F_ORDER, B_ORDER)[d][j]

            def mask_g(j):
                if j > 0:
                    pool.wait_ge(*dec_psum.at(layer, 3 * j - 1))
                both(lambda d, us: tt(b_g[:, us, :], dng[:, tile(j, d), us].unsqueeze(2).to_broadcast([P, DN_H, P]),
                                      (gt if d == 0 else lt).unsqueeze(1).to_broadcast([P, DN_H, P]), ALU.mult)).then_inc(gmask.sem, 1)

            def start_inverse(j):
                if j > 1:
                    pool.wait_ge(*s_psum.at(layer, j - 2))
                pool.tensor_copy(b_Y[j % 2][:, :, :], ident.unsqueeze(1).to_broadcast([P, UNITS, P])).then_inc(y_init.sem, 1)

            def mask_decays(j):
                pool.wait_ge(*dec_exp.at(layer, 3 * j + 2))
                link(both(lambda d, us: tt(b_D[:, us, :], b_D[:, us, :], (ge if d == 0 else le).unsqueeze(1).to_broadcast([P, DN_H, P]),
                                           ALU.mult)))

            def scale_state(j):
                pool.wait_ge(*v_psum.at(layer, 2 * j + 1))
                if wants_out(layer, j):
                    pool.wait_ge(*so_psum.at(layer, dn_i(layer, j, 2, 1, True)))
                if j > 0:
                    pool.wait_ge(*s_ready.at(layer, j - 1))
                for d in range(2):
                    q = slice(3 * d, 3 * d + 3)
                    ins = tt(S[:, q, :], S[:, q, :], egl[:, tile(j, d), q].unsqueeze(2).to_broadcast([P, 3, DN_D]), ALU.mult)
                ins.then_inc(s_scaled.sem, 1)

            mask_g(0)
            start_inverse(0)
            mask_decays(0)
            for j in range(STEPS):
                if j > 0:
                    pool.wait_ge(*inv_psum.at(layer, inv("y", j - 1, NL, 2)))
                both(lambda d, us: tt(b_nD[:, us, :], b_D[:, us, :], dnc[:, 0, tile(j, d), us].unsqueeze(2).to_broadcast([P, DN_H, P]),
                                      ALU.mult)).then_inc(dec_ready.sem, 1)
                if j > 0:
                    scale_state(j - 1)
                    pool.wait_ge(*s_psum.at(layer, j - 1))
                jobs = [(vb, 2, dnb[:, :, :]), (kbg, 1, dnc[:, 1]), (kdec, 1, dnx[:, 1])]
                if wants_out(layer, j):
                    jobs.append((qdec, 0, dnx[:, 0]))
                for dst, part, cf in jobs:
                    ins = both(lambda d, us: tt(dst[:, us, :], qkv[:, tile(j, d), part * DN_W:(part + 1) * DN_W]
                                                .rearrange("p (h d) -> p h d", d=DN_D),
                                                cf[:, tile(j, d), us].unsqueeze(2).to_broadcast([P, DN_H, DN_D]), ALU.mult))
                ins.then_inc(dn_prod.sem, 1)
                if j + 1 < STEPS:
                    mask_g(j + 1)
                    start_inverse(j + 1)
                    mask_decays(j + 1)
            scale_state(STEPS - 1)
            pool.wait_ge(*so_copied.all(layer))
            pool.wait_ge(*s_ready.at(layer, STEPS - 1))
            for t in range(nt):
                if t >= 2:
                    pool.wait_ge(*head_ss.at(layer, TILES + t - 2))
                tt(sq[:, t % 2, 0:640], ycat[:, t, 0:640], ycat[:, t, 0:640], ALU.mult).then_inc(head_sq.sem, 1)
            for t in range(nt):
                pool.wait_ge(*hn_mul.at(layer, t))
                a = ycat[:, t, 0:DN_W].rearrange("p (h d) -> p h d", d=DN_D)
                b = ycat[:, t, Y_DA:Y_WA].rearrange("p (h d) -> p h d", d=DA_V)
                link(tt(a, a, sm(layer, "dng").unsqueeze(1).to_broadcast([P, DN_H, DN_D]), ALU.mult))
                tt(a, a, gab[:, t, 0:DN_W].rearrange("p (h d) -> p h d", d=DN_D), ALU.mult)
                tt(b, b, gsub[:, layer, :].unsqueeze(1).to_broadcast([P, DA_H, DA_V]), ALU.mult).then_inc(y_done.sem, 1)

        def output(layer):
            nt = OUT_TILES[layer]
            n = 0
            for c in range(OUT_CH):
                for t in range(nt):
                    pool.wait_ge(*wo_scaled.at(layer, n))
                    v = x[:, t, c * 512:(c + 1) * 512]
                    tt(v, v, ycat[:, n % 2, 0:512], ALU.add).then_inc(x_mid.sem, 1)
                    n += 1

        def experts(layer):
            nt = OUT_TILES[layer]

            def scatter(done):
                for i in range(2):
                    for t in range(nt):
                        pool.indirect_dma_start(hs, bass.IndirectOffsetOnAxis(ap=pos[:, i, t:t + 1], axis=0),
                                                h2tok[:, t, :], None).then_inc(done, 16)

            pool.wait_ge(*pos_ready.at(layer, 0))
            pool.wait_ge(*h2tok_copied.all(layer))
            if layer == 0:
                pool.wait_ge(zero_in, 16 * ZERO_N)
            scatter(scattered)
            pool.wait_ge(*cmax_ready.at(layer, 0))
            most = pool.value_load(cmaxi[0:1, 0:1])
            sy = more[layer]
            with pool.If(most > CAP):
                for par in range(2):
                    pool.wait_ge(fast.out[par], (layer + 1) * SLOT_E)
                pool.memset(hg[:, 1, :], 0.0).then_inc(sy.cleared, 1)
                pool.wait_ge(sy.out, 16 * (ROUNDS[layer] - 1) * N_E)
                scatter(sy.scat)
            pool.wait_ge(*experts_done.at(layer, 0))

            def gather(rows):
                for t in range(nt):
                    if t >= 2:
                        pool.wait_ge(*x_next.at(layer, t - 2))
                    for i in range(2):
                        pool.indirect_dma_start(yab[:, t % 2, i, :], None, ys[0:rows, :],
                                                bass.IndirectOffsetOnAxis(ap=pos[:, i, t:t + 1], axis=0)).then_inc(gathered[t % 2], 16)

            with pool.If(most > CAP):
                gather(ROUNDS[layer] * N_E * CAP)
            with pool.If(most <= CAP):
                gather(N_E * CAP)

        for layer in range(DEPTH):
            ropes(layer)
            qk_norms(layer)
            deltanet(layer)
            output(layer)
            experts(layer)

    ctx.close()


INPUTS = ["x", "c", "ctx", "c_ctx", "ada_w", "ada_b", "norm1_g", "norm2_g", "w_in", "dn_conv_w", "dn_a_log", "dn_dt_bias",
          "dn_norm_g", "da_lambda", "da_subln_g", "wa_sink", "w_out", "router_group_w", "router_group_b",
          "router_expert_w", "router_expert_b", "exp_w_gate", "exp_w_up", "exp_w_down", "final_norm_g"]


def kernel(**inputs):
    import concourse.bacc as bacc
    from concourse.bass_utils import run_bass_kernel_spmd

    nc = bacc.Bacc("TRN2", target_bir_lowering=False, num_devices=1)
    arrays = {n: np.ascontiguousarray(inputs[n]) for n in INPUTS}
    arrays["tables"], arrays["levels"] = tables()
    arrays = {f"{n}_dram": a for n, a in arrays.items()}
    io = {n[:-5]: nc.dram_tensor(n, a.shape, mybir.dt.from_np(a.dtype), kind="ExternalInput").ap() for n, a in arrays.items()}
    out = nc.dram_tensor("out_dram", (1, SEQ, D), F32, kind="ExternalOutput").ap()
    backbone(nc, io, out)
    r = run_bass_kernel_spmd(nc, [arrays], core_ids=[0])
    return r.results[0]["out_dram"]
```
